# Optimizing a Trainium2 kernel written in Bass

```python
import jax, jax.numpy as jnp
from jax import lax
import numpy as np
import math

D_MODEL = 1024
BATCH = 1
SEQ = 1024
DEPTH = 2

CTX_LEN = 256
GRID_W = 64
Q_BLOCK = 128
ROPE_THETA = 10000.0
EPS = 1e-6

MLA_HEADS = 6
MLA_Q_RANK = 256
MLA_KV_RANK = 128
MLA_NOPE = 64
MLA_ROPE = 32
MLA_V = 64
MLA_WIDTH = MLA_HEADS * MLA_V
GQA_HEADS = 6
GQA_KV_HEADS = 2
GQA_HEAD_DIM = 64
GQA_WIDTH = GQA_HEADS * GQA_HEAD_DIM
CONV_CH = 256
CONV_K = 31
MIX_WIDTH = MLA_WIDTH + GQA_WIDTH + CONV_CH

L_MLA_KV = 0
L_MLA_KR = L_MLA_KV + MLA_KV_RANK
L_GQA_K = L_MLA_KR + MLA_ROPE
L_GQA_V = L_GQA_K + GQA_KV_HEADS * GQA_HEAD_DIM
KV_COLS = L_GQA_V + GQA_KV_HEADS * GQA_HEAD_DIM
OFF_MLA_Q = 0
OFF_KV = OFF_MLA_Q + MLA_Q_RANK
OFF_GQA_Q = OFF_KV + KV_COLS
OFF_CONV = OFF_GQA_Q + GQA_WIDTH
OFF_GATE = OFF_CONV + 2 * CONV_CH
IN_COLS = OFF_GATE + MIX_WIDTH


def rms_norm(x, g):
    xf = x.astype(jnp.float32)
    y = xf * lax.rsqrt(jnp.mean(xf * xf, axis=-1, keepdims=True) + EPS)
    return (y * g.astype(jnp.float32)).astype(x.dtype)

def layer_norm(x, g, b):
    xf = x.astype(jnp.float32)
    mu = jnp.mean(xf, axis=-1, keepdims=True)
    var = jnp.mean(jnp.square(xf - mu), axis=-1, keepdims=True)
    y = (xf - mu) * lax.rsqrt(var + EPS) * g.astype(jnp.float32) + b.astype(jnp.float32)
    return y.astype(x.dtype)

def rope_1d(x, pos):
    half = x.shape[-1] // 2
    freqs = ROPE_THETA ** (-jnp.arange(half, dtype=jnp.float32) / half)
    ang = pos.astype(jnp.float32)[:, None] * freqs[None, :]
    cos = jnp.cos(ang)[None, :, None, :]
    sin = jnp.sin(ang)[None, :, None, :]
    xf = x.astype(jnp.float32)
    x1, x2 = xf[..., :half], xf[..., half:]
    return jnp.concatenate([x1 * cos - x2 * sin, x1 * sin + x2 * cos], axis=-1).astype(x.dtype)

def axial_rope(x, row, col):
    r = x.shape[-1] // 2
    return jnp.concatenate([rope_1d(x[..., :r], row), rope_1d(x[..., r:], col)], axis=-1)

def block_attention(q, k, v):
    B, S, H, D = q.shape
    G = k.shape[2]
    R = H // G
    Dv = v.shape[-1]
    scale = D ** -0.5
    nblk = S // Q_BLOCK
    qb = q.reshape(B, nblk, Q_BLOCK, G, R, D).transpose(1, 0, 2, 3, 4, 5)

    def one_block(qi):
        s = jnp.einsum('bqgrd,bkgd->bgrqk', qi, k).astype(jnp.float32) * scale
        p = jax.nn.softmax(s, axis=-1).astype(v.dtype)
        return jnp.einsum('bgrqk,bkgv->bqgrv', p, v)

    o = lax.map(one_block, qb)
    return o.transpose(1, 0, 2, 3, 4, 5).reshape(B, S, H * Dv)

def mla_query(p, q_norm, w_uq, row, col):
    B, T = p.shape[:2]
    cq = rms_norm(p[..., OFF_MLA_Q:OFF_MLA_Q + MLA_Q_RANK], q_norm)
    q = (cq @ w_uq).reshape(B, T, MLA_HEADS, MLA_NOPE + MLA_ROPE)
    if row is not None:
        q = jnp.concatenate([q[..., :MLA_NOPE], axial_rope(q[..., MLA_NOPE:], row, col)], axis=-1)
    return q

def mla_keys_values(pkv, kv_norm, w_ukv, row, col):
    B, T = pkv.shape[:2]
    ckv = rms_norm(pkv[..., L_MLA_KV:L_MLA_KR], kv_norm)
    kv = (ckv @ w_ukv).reshape(B, T, MLA_HEADS, MLA_NOPE + MLA_V)
    k_nope, v = kv[..., :MLA_NOPE], kv[..., MLA_NOPE:]
    k_rope = pkv[..., L_MLA_KR:L_GQA_K][:, :, None, :]
    if row is not None:
        k_rope = axial_rope(k_rope, row, col)
    k_rope = jnp.broadcast_to(k_rope, (B, T, MLA_HEADS, MLA_ROPE))
    return jnp.concatenate([k_nope, k_rope], axis=-1), v

def gqa_query(p, q_norm, row, col):
    B, T = p.shape[:2]
    q = rms_norm(p[..., OFF_GQA_Q:OFF_CONV].reshape(B, T, GQA_HEADS, GQA_HEAD_DIM), q_norm)
    if row is not None:
        q = axial_rope(q, row, col)
    return q

def gqa_keys_values(pkv, k_norm, row, col):
    B, T = pkv.shape[:2]
    k = rms_norm(pkv[..., L_GQA_K:L_GQA_V].reshape(B, T, GQA_KV_HEADS, GQA_HEAD_DIM), k_norm)
    if row is not None:
        k = axial_rope(k, row, col)
    v = pkv[..., L_GQA_V:KV_COLS].reshape(B, T, GQA_KV_HEADS, GQA_HEAD_DIM)
    return k, v

def conformer_conv(u, dw_w, dw_b, ln_w, ln_b, pw_w, pw_b):
    a, g = jnp.split(u, 2, axis=-1)
    y = a * jax.nn.sigmoid(g)
    y = lax.conv_general_dilated(
        y, dw_w[:, None, :], window_strides=(1,),
        padding=((CONV_K // 2, CONV_K // 2),),
        dimension_numbers=('NWC', 'WIO', 'NWC'),
        feature_group_count=CONV_CH) + dw_b
    y = jax.nn.silu(layer_norm(y, ln_w, ln_b))
    return y @ pw_w + pw_b

def hybrid_layer(x, ctx, c, c_ctx, row, col, last,
                 norm_w, w_mod, b_mod, w_in, mla_q_norm, mla_w_uq, mla_kv_norm, mla_w_ukv,
                 gqa_q_norm, gqa_k_norm, conv_dw_w, conv_dw_b, conv_ln_w, conv_ln_b,
                 conv_pw_w, conv_pw_b, w_out):
    shift, scale, gate = jnp.split(jax.nn.silu(c) @ w_mod + b_mod, 3, axis=-1)
    shift_c, scale_c, gate_c = jnp.split(jax.nn.silu(c_ctx) @ w_mod + b_mod, 3, axis=-1)
    h = rms_norm(x, norm_w) * (1.0 + scale[:, None, :]) + shift[:, None, :]
    hc = rms_norm(ctx, norm_w) * (1.0 + scale_c) + shift_c

    p = h @ w_in
    if last:
        pc_kv = hc @ w_in[:, OFF_KV:OFF_GQA_Q]
    else:
        pc = hc @ w_in
        pc_kv = pc[..., OFF_KV:OFF_GQA_Q]
    p_kv = p[..., OFF_KV:OFF_GQA_Q]

    k_mla_c, v_mla_c = mla_keys_values(pc_kv, mla_kv_norm, mla_w_ukv, None, None)
    k_gqa_c, v_gqa_c = gqa_keys_values(pc_kv, gqa_k_norm, None, None)

    k_mla, v_mla = mla_keys_values(p_kv, mla_kv_norm, mla_w_ukv, row, col)
    q_mla = mla_query(p, mla_q_norm, mla_w_uq, row, col)
    o_mla = block_attention(q_mla, jnp.concatenate([k_mla, k_mla_c], axis=1),
                            jnp.concatenate([v_mla, v_mla_c], axis=1))
    k_gqa, v_gqa = gqa_keys_values(p_kv, gqa_k_norm, row, col)
    q_gqa = gqa_query(p, gqa_q_norm, row, col)
    o_gqa = block_attention(q_gqa, jnp.concatenate([k_gqa, k_gqa_c], axis=1),
                            jnp.concatenate([v_gqa, v_gqa_c], axis=1))
    o_conv = conformer_conv(p[..., OFF_CONV:OFF_GATE], conv_dw_w, conv_dw_b,
                            conv_ln_w, conv_ln_b, conv_pw_w, conv_pw_b)
    y = jnp.concatenate([o_mla, o_gqa, o_conv], axis=-1) * jax.nn.silu(p[..., OFF_GATE:])
    x_new = x + gate[:, None, :] * (y @ w_out)

    if last:
        return x_new, ctx

    oc_mla = block_attention(mla_query(pc, mla_q_norm, mla_w_uq, None, None), k_mla_c, v_mla_c)
    oc_gqa = block_attention(gqa_query(pc, gqa_q_norm, None, None), k_gqa_c, v_gqa_c)
    oc_conv = conformer_conv(pc[..., OFF_CONV:OFF_GATE], conv_dw_w, conv_dw_b,
                             conv_ln_w, conv_ln_b, conv_pw_w, conv_pw_b)
    yc = jnp.concatenate([oc_mla, oc_gqa, oc_conv], axis=-1) * jax.nn.silu(pc[..., OFF_GATE:])
    ctx_new = ctx + gate_c * (yc @ w_out)
    return x_new, ctx_new

def first_inputs(seed: int = 0) -> dict:
    key = jax.random.key(seed)
    ks = jax.random.split(key, 24)
    f32 = jnp.float32
    nrm = lambda k, shape, s: jax.random.normal(k, shape, f32) * s
    L, D = DEPTH, D_MODEL
    return {
        'x': nrm(ks[0], (BATCH, SEQ, D), 1.0),
        'c': nrm(ks[1], (BATCH, D), 1.0),
        'ctx': nrm(ks[2], (BATCH, CTX_LEN, D), 1.0),
        'c_ctx': nrm(ks[3], (D,), 1.0),
        'norm_w': 1.0 + nrm(ks[4], (L, D), 0.05),
        'w_mod': nrm(ks[5], (L, D, 3 * D), 0.5 * D ** -0.5),
        'b_mod': nrm(ks[6], (L, 3 * D), 0.02),
        'w_in': nrm(ks[7], (L, D, IN_COLS), D ** -0.5),
        'mla_q_norm': 1.0 + nrm(ks[8], (L, MLA_Q_RANK), 0.05),
        'mla_w_uq': nrm(ks[9], (L, MLA_Q_RANK, MLA_HEADS * (MLA_NOPE + MLA_ROPE)), MLA_Q_RANK ** -0.5),
        'mla_kv_norm': 1.0 + nrm(ks[10], (L, MLA_KV_RANK), 0.05),
        'mla_w_ukv': nrm(ks[11], (L, MLA_KV_RANK, MLA_HEADS * (MLA_NOPE + MLA_V)), MLA_KV_RANK ** -0.5),
        'gqa_q_norm': 1.0 + nrm(ks[12], (L, GQA_HEAD_DIM), 0.05),
        'gqa_k_norm': 1.0 + nrm(ks[13], (L, GQA_HEAD_DIM), 0.05),
        'conv_dw_w': nrm(ks[14], (L, CONV_K, CONV_CH), CONV_K ** -0.5),
        'conv_dw_b': nrm(ks[15], (L, CONV_CH), 0.02),
        'conv_ln_w': 1.0 + nrm(ks[16], (L, CONV_CH), 0.05),
        'conv_ln_b': nrm(ks[17], (L, CONV_CH), 0.02),
        'conv_pw_w': nrm(ks[18], (L, CONV_CH, CONV_CH), CONV_CH ** -0.5),
        'conv_pw_b': nrm(ks[19], (L, CONV_CH), 0.02),
        'w_out': nrm(ks[20], (L, MIX_WIDTH, D), MIX_WIDTH ** -0.5),
        'final_norm_w': 1.0 + nrm(ks[21], (D,), 0.05),
    }

def first_block(x, c, ctx, c_ctx, norm_w, w_mod, b_mod, w_in, mla_q_norm, mla_w_uq, mla_kv_norm,
              mla_w_ukv, gqa_q_norm, gqa_k_norm, conv_dw_w, conv_dw_b, conv_ln_w, conv_ln_b,
              conv_pw_w, conv_pw_b, w_out, final_norm_w):
    S = x.shape[1]
    rows = S // GRID_W
    row = jnp.repeat(jnp.arange(rows, dtype=jnp.int32), GRID_W)
    col = jnp.tile(jnp.arange(GRID_W, dtype=jnp.int32), rows)
    for l in range(DEPTH):
        x, ctx = hybrid_layer(
            x, ctx, c, c_ctx, row, col, l == DEPTH - 1,
            norm_w[l], w_mod[l], b_mod[l], w_in[l], mla_q_norm[l], mla_w_uq[l],
            mla_kv_norm[l], mla_w_ukv[l], gqa_q_norm[l], gqa_k_norm[l],
            conv_dw_w[l], conv_dw_b[l], conv_ln_w[l], conv_ln_b[l],
            conv_pw_w[l], conv_pw_b[l], w_out[l])
    return rms_norm(x, final_norm_w)


DEPTH_2 = 1

PLE_DIM = 256
GLA_HEADS = 4
GLA_DK = D_MODEL // 2 // GLA_HEADS
GLA_DV = D_MODEL // GLA_HEADS
GLA_GATE_RANK = 16
GLA_GATE_TEMP = 16.0
GLA_CHUNK = 64
DSA_HEADS = 16
DSA_HEAD_DIM = D_MODEL // DSA_HEADS
DSA_LATENT = 128
IDX_HEADS = 8
IDX_DIM = 64
TOPK_MAX = 256
D_FF = 2816
CONV_W = 3
LN_EPS = 1e-5
DEEPNORM_ALPHA = (2.0 * DEPTH_2) ** 0.25
DEEPNORM_BETA = (8.0 * DEPTH_2) ** -0.25
SPLIT_SIZES = (
    GLA_HEADS * GLA_DK,
    GLA_HEADS * GLA_DK,
    GLA_HEADS * GLA_DV,
    GLA_HEADS * GLA_DV,
    GLA_GATE_RANK,
    DSA_HEADS * DSA_LATENT,
    DSA_LATENT,
    IDX_HEADS * IDX_DIM,
    IDX_DIM,
    IDX_HEADS,
    2 * D_MODEL,
)
IN_COLS_2 = sum(SPLIT_SIZES)


def _split_points():
    return [int(v) for v in np.cumsum(np.array(SPLIT_SIZES))[:-1]]

def layer_norm_2(x, g, b):
    xf = x.astype(jnp.float32)
    mu = jnp.mean(xf, axis=-1, keepdims=True)
    var = jnp.mean(jnp.square(xf - mu), axis=-1, keepdims=True)
    return ((xf - mu) * lax.rsqrt(var + LN_EPS) * g.astype(jnp.float32) + b.astype(jnp.float32)).astype(x.dtype)

def rms_norm_2(x, g):
    xf = x.astype(jnp.float32)
    ms = jnp.mean(jnp.square(xf), axis=-1, keepdims=True)
    return (xf * lax.rsqrt(ms + LN_EPS) * g.astype(jnp.float32)).astype(x.dtype)

def gla_chunked(q, k, v, log_a):
    q, k, v, log_a = (t.astype(jnp.float32) for t in (q, k, v, log_a))
    B, L, H, dk = q.shape
    dv = v.shape[-1]
    C = GLA_CHUNK
    N = L // C

    def to_chunks(t):
        return t.reshape(B, N, C, H, t.shape[-1]).transpose(1, 0, 3, 2, 4)

    qc, kc, vc, ac = (to_chunks(t) for t in (q, k, v, log_a))
    b = jnp.cumsum(ac, axis=3)
    b_last = b[:, :, :, -1:, :]
    q_in = qc * jnp.exp(b)
    k_in = kc * jnp.exp(-b)
    k_state = kc * jnp.exp(b_last - b)
    causal = jnp.tril(jnp.ones((C, C), dtype=bool))
    attn = jnp.where(causal, jnp.einsum('nbhid,nbhjd->nbhij', q_in, k_in), 0.0)
    o_intra = jnp.einsum('nbhij,nbhjv->nbhiv', attn, vc)

    def step(S, xs):
        q_i, k_i, v_i, decay_i = xs
        o = jnp.einsum('bhid,bhdv->bhiv', q_i, S)
        S = S * decay_i[:, :, 0, :, None] + jnp.einsum('bhjd,bhjv->bhdv', k_i, v_i)
        return S, o

    S0 = jnp.zeros((B, H, dk, dv), jnp.float32)
    _, o_inter = lax.scan(step, S0, (q_in, k_state, vc, jnp.exp(b_last)))
    o = o_intra + o_inter
    return o.transpose(1, 0, 3, 2, 4).reshape(B, L, H, dv)

def dsa_attention(q, ckv, iq, ik, iw):
    B, L, H, dc = q.shape
    top_k = min(TOPK_MAX, L // 4)
    nb = L // Q_BLOCK
    key_pos = jnp.arange(L, dtype=jnp.int32)

    def blockify(t):
        return jnp.swapaxes(t.reshape((B, nb, Q_BLOCK) + t.shape[2:]), 0, 1)

    def one_block(args):
        q_b, iq_b, iw_b, q_pos = args
        s = jax.nn.relu(jnp.einsum('bqhd,bsd->bqhs', iq_b, ik).astype(jnp.float32))
        score = jnp.einsum('bqh,bqhs->bqs', iw_b.astype(jnp.float32), s)
        causal = key_pos[None, :] <= q_pos[:, None]
        score = jnp.where(causal[None], score, -jnp.inf)
        _, idx = lax.top_k(score, top_k)
        valid = idx <= q_pos[None, :, None]
        kv_sel = jax.vmap(lambda c, i: c[i])(ckv, idx)
        logits = jnp.einsum('bqhc,bqkc->bqhk', q_b, kv_sel).astype(jnp.float32) * (dc ** -0.5)
        logits = jnp.where(valid[:, :, None, :], logits, -jnp.inf)
        probs = jax.nn.softmax(logits, axis=-1).astype(kv_sel.dtype)
        return jnp.einsum('bqhk,bqkc->bqhc', probs, kv_sel)

    pos_blocks = jnp.arange(L, dtype=jnp.int32).reshape(nb, Q_BLOCK)
    out = lax.map(one_block, (blockify(q), blockify(iq), blockify(iw), pos_blocks))
    return jnp.swapaxes(out, 0, 1).reshape(B, L, H, dc)

def causal_dwconv(h, w, b):
    L = h.shape[1]
    hp = jnp.pad(h, ((0, 0), (CONV_W - 1, 0), (0, 0)))
    out = w[CONV_W - 1] * h
    for j in range(CONV_W - 1):
        out = out + w[j] * hp[:, j:j + L]
    return out + b

def second_inputs(seed: int = 0) -> dict:
    key = jax.random.key(seed)
    ks = jax.random.split(key, 24)

    def nrm(k, shape, fan_in, scale=1.0):
        return jax.random.normal(k, shape, jnp.float32) * (scale * fan_in ** -0.5)

    def gain(k, shape):
        return 1.0 + 0.02 * jax.random.normal(k, shape, jnp.float32)

    def bias(k, shape, s=0.02):
        return s * jax.random.normal(k, shape, jnp.float32)

    return {
        'x': jax.random.normal(ks[0], (BATCH, SEQ, D_MODEL), jnp.float32),
        'p': jax.random.normal(ks[1], (DEPTH_2, BATCH, SEQ, PLE_DIM), jnp.float32),
        'w_in': nrm(ks[2], (DEPTH_2, D_MODEL, IN_COLS_2), D_MODEL),
        'w_gla_gate_up': nrm(ks[3], (DEPTH_2, GLA_GATE_RANK, GLA_HEADS * GLA_DK), GLA_GATE_RANK),
        'b_gla_gate': bias(ks[4], (DEPTH_2, GLA_HEADS * GLA_DK), 0.1),
        'g_gla_norm': gain(ks[5], (DEPTH_2, GLA_HEADS * GLA_DV)),
        'w_gla_proj': nrm(ks[6], (DEPTH_2, GLA_HEADS * GLA_DV, D_MODEL), GLA_HEADS * GLA_DV),
        'g_ckv_norm': gain(ks[7], (DEPTH_2, DSA_LATENT)),
        'w_uv': nrm(ks[8], (DEPTH_2, DSA_HEADS, DSA_LATENT, DSA_HEAD_DIM), DSA_LATENT),
        'w_dsa_proj': nrm(ks[9], (DEPTH_2, DSA_HEADS * DSA_HEAD_DIM, D_MODEL), DSA_HEADS * DSA_HEAD_DIM),
        'w_out': nrm(ks[10], (DEPTH_2, D_MODEL, D_MODEL), D_MODEL, DEEPNORM_BETA),
        'ln1_g': gain(ks[11], (DEPTH_2, D_MODEL)),
        'ln1_b': bias(ks[12], (DEPTH_2, D_MODEL)),
        'w_up': nrm(ks[13], (DEPTH_2, D_MODEL, 2 * D_FF), D_MODEL),
        'conv_w': nrm(ks[14], (DEPTH_2, CONV_W, 2 * D_FF), CONV_W),
        'conv_b': bias(ks[15], (DEPTH_2, 2 * D_FF)),
        'w_down': nrm(ks[16], (DEPTH_2, D_FF, D_MODEL), D_FF, DEEPNORM_BETA),
        'ln2_g': gain(ks[17], (DEPTH_2, D_MODEL)),
        'ln2_b': bias(ks[18], (DEPTH_2, D_MODEL)),
        'w_ple': nrm(ks[19], (DEPTH_2, PLE_DIM, D_MODEL), PLE_DIM, DEEPNORM_BETA),
        'w_ple_gate': nrm(ks[20], (DEPTH_2, D_MODEL, D_MODEL), D_MODEL),
        'ln3_g': gain(ks[21], (DEPTH_2, D_MODEL)),
        'ln3_b': bias(ks[22], (DEPTH_2, D_MODEL)),
    }

def second_block(x, p, w_in, w_gla_gate_up, b_gla_gate, g_gla_norm, w_gla_proj, g_ckv_norm, w_uv,
              w_dsa_proj, w_out, ln1_g, ln1_b, w_up, conv_w, conv_b, w_down, ln2_g, ln2_b,
              w_ple, w_ple_gate, ln3_g, ln3_b):
    B, L, _ = x.shape
    for i in range(DEPTH_2):
        proj = x @ w_in[i]
        gq, gk, gv, gr, ga, dq, ckv, iq, ik, iw, gates = jnp.split(proj, _split_points(), axis=-1)

        q_a = gq.reshape(B, L, GLA_HEADS, GLA_DK) * (GLA_DK ** -0.5)
        k_a = gk.reshape(B, L, GLA_HEADS, GLA_DK)
        v_a = gv.reshape(B, L, GLA_HEADS, GLA_DV)
        z = (ga @ w_gla_gate_up[i] + b_gla_gate[i]).astype(jnp.float32)
        log_a = (jax.nn.log_sigmoid(z) / GLA_GATE_TEMP).reshape(B, L, GLA_HEADS, GLA_DK)
        o_a = gla_chunked(q_a, k_a, v_a, log_a)
        o_a = rms_norm_2(o_a, g_gla_norm[i].reshape(GLA_HEADS, GLA_DV))
        o_a = o_a.reshape(B, L, GLA_HEADS * GLA_DV).astype(x.dtype) * jax.nn.silu(gr)
        y_a = o_a @ w_gla_proj[i]

        q_b = dq.reshape(B, L, DSA_HEADS, DSA_LATENT)
        c_kv = rms_norm_2(ckv, g_ckv_norm[i])
        iq_b = iq.reshape(B, L, IDX_HEADS, IDX_DIM)
        iw_b = iw * ((IDX_HEADS ** -0.5) * (IDX_DIM ** -0.5))
        o_b = dsa_attention(q_b, c_kv, iq_b, ik, iw_b)
        o_b = jnp.einsum('blhc,hcd->blhd', o_b, w_uv[i]).reshape(B, L, DSA_HEADS * DSA_HEAD_DIM)
        y_b = o_b @ w_dsa_proj[i]

        gate_a, gate_b = jnp.split(gates, 2, axis=-1)
        mixed = (jax.nn.sigmoid(gate_a) * y_a + jax.nn.sigmoid(gate_b) * y_b) @ w_out[i]
        x = layer_norm_2(DEEPNORM_ALPHA * x + mixed, ln1_g[i], ln1_b[i])

        h = causal_dwconv(x @ w_up[i], conv_w[i], conv_b[i])
        h_gate, h_val = jnp.split(h, 2, axis=-1)
        ffn = (jax.nn.silu(h_gate) * h_val) @ w_down[i]
        x = layer_norm_2(DEEPNORM_ALPHA * x + ffn, ln2_g[i], ln2_b[i])

        ple = jax.nn.sigmoid(x @ w_ple_gate[i]) * (p[i] @ w_ple[i])
        x = layer_norm_2(DEEPNORM_ALPHA * x + ple, ln3_g[i], ln3_b[i])
    return x


_first_inputs = second_inputs


def second_inputs(seed=0):
    import zlib

    import numpy as np

    out = dict(_first_inputs(seed))
    spreads = {}
    factors = {'w_gla_gate_up': 3.213,
     'b_gla_gate': 7.922,
     'g_gla_norm': 33.188,
     'g_ckv_norm': 8.0,
     'ln1_g': 2.797,
     'ln1_b': 2.857,
     'conv_b': 7.104,
     'ln2_g': 8.566,
     'ln2_b': 8.629,
     'ln3_g': 7.546,
     'ln3_b': 7.771}
    for name, (base, spread) in spreads.items():
        noise = np.random.default_rng([zlib.crc32(name.encode()), seed]).standard_normal(out[name].shape)
        drawn = base * np.exp(spread * noise) if base else spread * noise
        out[name] = __import__('jax').numpy.asarray(drawn.astype(out[name].dtype))
    for name, factor in factors.items():
        out[name] = (out[name] * factor).astype(out[name].dtype)
    return out


_narrow_inputs = second_inputs


def second_inputs(seed=0):

    out = dict(_narrow_inputs(seed))
    wider = {'ln2_g': 3.24, 'ln2_b': 3.24, 'ln3_g': 3.09, 'ln3_b': 3.09}
    for name, times in wider.items():
        mean = out[name].mean()
        out[name] = (mean + times * (out[name] - mean)).astype(out[name].dtype)
    return out


def setup_inputs(seed=0):
    out = dict(first_inputs(seed))
    for name, value in second_inputs(seed + 1).items():
        if name != "x":
            out[name + "_2"] = value
    return out


def reference(
    x, c, ctx, c_ctx, norm_w, w_mod, b_mod, w_in, mla_q_norm, mla_w_uq, mla_kv_norm, mla_w_ukv,
    gqa_q_norm, gqa_k_norm, conv_dw_w, conv_dw_b, conv_ln_w, conv_ln_b, conv_pw_w, conv_pw_b,
    w_out, final_norm_w, p_2, w_in_2, w_gla_gate_up_2, b_gla_gate_2, g_gla_norm_2, w_gla_proj_2,
    g_ckv_norm_2, w_uv_2, w_dsa_proj_2, w_out_2, ln1_g_2, ln1_b_2, w_up_2, conv_w_2, conv_b_2,
    w_down_2, ln2_g_2, ln2_b_2, w_ple_2, w_ple_gate_2, ln3_g_2, ln3_b_2,
):
    x = first_block(
        x, c, ctx, c_ctx, norm_w, w_mod, b_mod, w_in, mla_q_norm, mla_w_uq, mla_kv_norm,
        mla_w_ukv, gqa_q_norm, gqa_k_norm, conv_dw_w, conv_dw_b, conv_ln_w, conv_ln_b,
        conv_pw_w, conv_pw_b, w_out, final_norm_w,
    )
    return second_block(
        x, p_2, w_in_2, w_gla_gate_up_2, b_gla_gate_2, g_gla_norm_2, w_gla_proj_2, g_ckv_norm_2,
        w_uv_2, w_dsa_proj_2, w_out_2, ln1_g_2, ln1_b_2, w_up_2, conv_w_2, conv_b_2, w_down_2,
        ln2_g_2, ln2_b_2, w_ple_2, w_ple_gate_2, ln3_g_2, ln3_b_2,
    )


_drawn_inputs = setup_inputs


def setup_inputs(seed=0):
    import zlib

    import numpy as np

    out = dict(_drawn_inputs(seed))
    spreads = {}
    factors = {'mla_q_norm': 4.603,
     'gqa_q_norm': 4.983,
     'gqa_k_norm': 6.175,
     'conv_ln_b': 3.0,
     'g_ckv_norm_2': 2.962,
     'g_gla_norm_2': 3.562}
    for name, (base, spread) in spreads.items():
        noise = np.random.default_rng([zlib.crc32(name.encode()), seed]).standard_normal(out[name].shape)
        drawn = base * np.exp(spread * noise) if base else spread * noise
        out[name] = __import__('jax').numpy.asarray(drawn.astype(out[name].dtype))
    for name, factor in factors.items():
        out[name] = (out[name] * factor).astype(out[name].dtype)
    return out
```

```python
from contextlib import ExitStack, contextmanager

import numpy as np

import concourse.bass as bass
from concourse import mybir

F32 = mybir.dt.float32
ACT = mybir.ActivationFunctionType
ALU = mybir.AluOpType
AX = mybir.AxisListType

P = 128
D = 1024
KD = D // P
T = 1024
C = 256
TC = T + C
LAYERS = 2
THETA = 10000.0
GRID_W = 64
EPS = 1e-6
MH, MNOPE, MROPE, MV = 6, 64, 32, 64
MQ = MNOPE + MROPE
GH, GKV, GD = 6, 2, 64
CC, CK = 256, 31
PAD = CK // 2
GQA_ORDER = [0, 3, 1, 4, 2, 5]

LN_EPS = 1e-5
ALPHA = 2.0 ** 0.25
GLH, GDK, GDV, GRANK, GTEMP = 4, 128, 256, 16, 16.0
DH, DL, DHD = 16, 128, 64
IH, ID_ = 8, 64
TOPK = 256
FF = 2816
KF = FF // P
PLE = 256
QT = T // P
NEG = -1.0e30
LOW = -3.0e38


def first_columns():
    q, kv = 0, 256
    kr, gk, gv = kv + 128, kv + 160, kv + 288
    gq = kv + 416
    conv = gq + 384
    gate = conv + 512
    return q, kv, kr, gk, gv, gq, conv, gate


def mix_order():
    order = list(range(MH * MV))
    for h in GQA_ORDER:
        order += list(range(384 + 64 * h, 384 + 64 * h + 64))
    return np.array(order + list(range(768, 1024)))


def second_columns():
    sizes = [512, 512, 1024, 1024, 16, 2048, 128, 512, 64, 8, 2048]
    return dict(zip("gq gk gv gr ga dq ckv iq ik iw gates".split(), np.concatenate([[0], np.cumsum(sizes)[:-1]]).tolist()))


def column_block(w, cols):
    a = w[:, cols] if not isinstance(cols, int) else w[:, cols:cols + P]
    return a.reshape(-1, P, P).transpose(1, 0, 2).reshape(P, -1)


def block_plan():
    plan, n = {}, 0
    counts = [("mod", LAYERS * 24)]
    for l in range(LAYERS):
        counts += [(f"kv{l}", 4), (f"q{l}", 5), (f"conv{l}", 4), (f"gate{l}", 8), (f"out{l}", 8)]
    counts += [("index", 6), ("gates_a", 8), ("gr", 8), ("gla", 16), ("gla_out", 8),
               ("dsa", 16), ("mix", 16), ("out2", 8), ("up", 44), ("down", 24), ("ple", 16)]
    for name, k in counts:
        plan[name] = n
        n += k
    return plan, n


BLOCKS, NBLOCKS = block_plan()

def offsets(**sizes):
    at, n = {}, 0
    for name, size in sizes.items():
        at[name] = n
        n += size
    return at, n


CON, NCON = offsets(ident=P, ones=P, halves=P, turn_mla=MROPE, turn_gqa=P, b_mod=LAYERS * 24, final_w=KD, vec=2 * KD, tri=P, later=P)
TAB, NTAB = offsets(mla_cos=T, mla_sin=T, gqa_cos=T, gqa_sin=T)
PA, NPA = offsets(uqk=MH * 256, uv=MH * MV, dw=2 * CK, dwb=2, lnw=2, lnb=2, pw=2 * CC, pwb=2, nw=KD, qn=2, kvn=1, gqn=1, gkn=1)
PB, NPB = offsets(gate_up=512, b_gate=4, gla_n=8, ckv_n=1, uv=DH * DHD, ln1g=8, ln1b=8, cw=3 * 2 * KF, cb=2 * KF,
                  ln2g=8, ln2b=8, ln3g=8, ln3b=8)

W_AT = 0
CON_AT = W_AT + 2 * 1024
PAR_AT = CON_AT + NCON
STAT_AT = PAR_AT + max(NPA, NPB)
MOD_AT = STAT_AT + TC
GAIN_AT = MOD_AT + LAYERS * 48
SMALL_AT = GAIN_AT + 2 * KD
FREE_AT = SMALL_AT + 64
H_AT = FREE_AT
VM_AT = H_AT
VG_AT = VM_AT + 10 * MH * MV
KG_AT = VG_AT + 10 * P
KM_AT = KG_AT + 2 * TC
Y_AT = H_AT + KD * TC
RAW_AT = Y_AT + KD * TC
CKV_AT, KR_AT, GK_AT, GV_AT, CQ_AT, GQ_AT = (RAW_AT + i * TC for i in (0, 1, 2, 3, 4, 6))
U_AT = RAW_AT + 9 * TC
U_SEG = T + 2 * PAD
U_LEN = U_SEG + C + 2 * PAD
QM_AT = U_AT
TAB_AT = U_AT + 2 * U_LEN
TMP_AT = TAB_AT + NTAB
ACC_AT = TMP_AT + 2 * TC
HW_AT = TMP_AT + 4 * TC
QS_AT = HW_AT + 512
OT_AT = QS_AT + 256
END1 = OT_AT + P
X_AT = H_AT
GAP_AT = H_AT + T
MIX_AT = X_AT + KD * TC
GR_AT = MIX_AT + KD * T
MASK_AT = GR_AT + KD * T
MISC_AT = MASK_AT + QT * (QT + 1) // 2 * P
IW_AT = MISC_AT + T
CL_AT = IW_AT + QT * IH
CLT_AT = CL_AT + T
GLA_Q, GLA_K, GLA_KS, GLA_E, GLA_S = (CLT_AT + (i + 1) * T for i in range(5))
GLA_B, GLA_L, GLA_O = TMP_AT, TMP_AT + T, TMP_AT + 2 * T
GLA_SM = GLA_O + 2 * T
GLA_SMALL = GLA_SM + GDV
QD_AT = CLT_AT + T
OL_AT = QD_AT + 2 * T
A_AT = X_AT + KD * TC
HG_AT = A_AT + KF * T
PT_IN_AT = HG_AT + 2 * T
ARENA = 53000
assert END1 <= ARENA and GLA_S + GDV <= TMP_AT and OL_AT + 2 * T <= TMP_AT + 300 and PT_IN_AT + 2 * T <= TMP_AT


def mask_at(t):
    return MASK_AT + t * (t + 1) // 2 * P


SLOT = 1536
BANK6, BANK7 = 3072, 3584


def chunks(n, start=0):
    return [(c, min(512, start + n - c)) for c in range(start, start + n, 512)]


class Event:

    def __init__(self, name, sem, unit=1):
        self.name, self.sem, self.unit = name, sem, unit


class Track:

    def __init__(self, eng, name, step=None, waited=None):
        self.eng, self.step, self.name, self.got, self.loops = eng, step, name, {}, []
        self.waited = waited
        self.tiles = 0

    def alone(self):
        if self.loops:
            self.eng.sem_inc(self.waited.sem, 1)

    def next(self, ev, n=1):
        self.got[ev.name] = self.got.get(ev.name, 0) + n
        value = self.got[ev.name] * ev.unit
        for i, per in self.loops:
            if per.get(ev.name, 0):
                value = value + i * (per[ev.name] * ev.unit)
        return value

    @contextmanager
    def loop(self, n, name):
        name = f"{self.name}_{name}"
        per = PASSES.get(name, {})
        before = dict(self.got)
        with self.eng.Fori(0, n) as i:
            self.loops.append((i, per))
            yield i
            self.loops.pop()
        one = {k: v - before.get(k, 0) for k, v in self.got.items() if v != before.get(k, 0)}
        assert one == per, (name, one, per)
        for k, v in one.items():
            self.got[k] = before.get(k, 0) + n * v


PASSES = {
    "sp_stream": dict(block_done_0=1, block_done_1=1),
    "pe_mod": dict(w_loaded_0=1, psum_free_0=1, w_loaded_1=1, psum_free_1=1),
    "pe_kv0": dict(w_loaded_0=1, psum_free_0=1, w_loaded_1=1, psum_free_1=1),
    "pe_q0": dict(w_loaded_0=1, psum_free_0=1, w_loaded_1=1, psum_free_1=1),
    "pe_gate0": dict(w_loaded_0=1, psum_free_0=1, w_loaded_1=1, psum_free_1=1),
    "pe_mla_x0": dict(q_ready_0=1, q_ready_1=1, p_ready_0=1, ot_used=1, t_moved_0=2, t_moved_1=2, t_moved_2=2, p_ready_1=1, o_moved=2),
    "pe_mla_c0": dict(q_ready_0=1, q_ready_1=1, p_ready_0=1, ot_used=1, t_moved_0=2, p_ready_1=1, o_moved=2),
    "pe_mla0": dict(stage_pe=2, stage_act=2, stage_dve=2, hw_ready_0=1, hw_ready_1=1, prep_moved_0=2, prep_moved_1=2, q_ready_0=10, q_ready_1=10, p_ready_0=10, ot_used=10, t_moved_0=20, t_moved_1=16, t_moved_2=16, p_ready_1=10, o_moved=20),
    "pe_gqa_x0": dict(q_ready_0=1, q_ready_1=1, p_ready_0=1, ot_used=1, t_moved_0=2, t_moved_1=2, t_moved_2=2, p_ready_1=1, o_moved=2),
    "pe_gqa_c0": dict(q_ready_0=1, q_ready_1=1, p_ready_0=1, ot_used=1, t_moved_0=2, p_ready_1=1, o_moved=2),
    "pe_gqa0": dict(q_ready_0=10, q_ready_1=10, p_ready_0=10, ot_used=10, t_moved_0=20, t_moved_1=16, t_moved_2=16, p_ready_1=10, o_moved=20),
    "pe_out0": dict(w_loaded_0=1, psum_free_0=1, w_loaded_1=1, psum_free_1=1),
    "pe_kv1": dict(w_loaded_0=1, psum_free_0=1, w_loaded_1=1, psum_free_1=1),
    "pe_q1": dict(w_loaded_0=1, psum_free_0=1, w_loaded_1=1, psum_free_1=1),
    "pe_gate1": dict(w_loaded_0=1, psum_free_0=1, w_loaded_1=1, psum_free_1=1),
    "pe_mla_x1": dict(q_ready_0=1, q_ready_1=1, p_ready_0=1, ot_used=1, t_moved_0=2, t_moved_1=2, t_moved_2=2, p_ready_1=1, o_moved=2),
    "pe_mla1": dict(stage_pe=2, stage_act=2, stage_dve=2, hw_ready_0=1, hw_ready_1=1, prep_moved_0=2, prep_moved_1=2, q_ready_0=8, q_ready_1=8, p_ready_0=8, ot_used=8, t_moved_0=16, t_moved_1=16, t_moved_2=16, p_ready_1=8, o_moved=16),
    "pe_gqa_x1": dict(q_ready_0=1, q_ready_1=1, p_ready_0=1, ot_used=1, t_moved_0=2, t_moved_1=2, t_moved_2=2, p_ready_1=1, o_moved=2),
    "pe_gqa1": dict(q_ready_0=8, q_ready_1=8, p_ready_0=8, ot_used=8, t_moved_0=16, t_moved_1=16, t_moved_2=16, p_ready_1=8, o_moved=16),
    "pe_out1": dict(w_loaded_0=1, psum_free_0=1, w_loaded_1=1, psum_free_1=1),
    "pe_index": dict(w_loaded_0=1, psum_free_0=1, w_loaded_1=1, psum_free_1=1),
    "pe_index2": dict(q_ready_0=1, q_ready_1=1),
    "pe_index3": dict(q_ready_0=1, q_ready_1=1),
    "pe_index4": dict(q_ready_0=1, q_ready_1=1),
    "pe_index5": dict(q_ready_0=1, q_ready_1=1),
    "pe_index6": dict(q_ready_0=1, q_ready_1=1),
    "pe_index7": dict(q_ready_0=1, q_ready_1=1),
    "pe_gates_a": dict(w_loaded_0=1, psum_free_0=1, w_loaded_1=1, psum_free_1=1),
    "pe_gr": dict(w_loaded_0=1, psum_free_0=1, w_loaded_1=1, psum_free_1=1),
    "pe_gla": dict(act_to_pe=1, w_loaded_0=2, psum_free_0=2, w_loaded_1=2, psum_free_1=2, stage_pe=4, stage_act=4, stage_dve=4, scaled_state=7, state_ready=7, chunk_moved=8),
    "pe_gla_out": dict(w_loaded_0=1, psum_free_0=1, w_loaded_1=1, psum_free_1=1),
    "pe_dsa": dict(w_loaded_0=1, psum_free_0=1, w_loaded_1=1, psum_free_1=1, stage_pe=3, stage_act=3, stage_dve=3, q_ready_0=8, q_ready_1=8, p_ready_0=8, ot_used=16, t_moved_0=16, t_moved_1=8, t_moved_2=4, p_ready_1=8, o_moved=16),
    "pe_mix": dict(w_loaded_0=1, psum_free_0=1, w_loaded_1=1, psum_free_1=1),
    "pe_out2": dict(w_loaded_0=1, psum_free_0=1, w_loaded_1=1, psum_free_1=1),
    "pe_up": dict(w_loaded_0=1, psum_free_0=1, w_loaded_1=1, psum_free_1=1),
    "pe_down": dict(w_loaded_0=3, psum_free_0=1, w_loaded_1=3, psum_free_1=1),
    "pe_ple": dict(w_loaded_0=1, psum_free_0=1, w_loaded_1=1, psum_free_1=1),
    "act_mla_x0": dict(mx_ready_0=1, t_done_1=2, mx_ready_1=1, o_done=2, r_ready_0=1, r_ready_1=1),
    "act_mla_c0": dict(mx_ready_0=1, mx_ready_1=1, o_done=2, r_ready_0=1, r_ready_1=1),
    "act_mla0": dict(stage_pe=2, stage_act=2, stage_dve=2, proj_done_0=2, proj_done_1=2, mx_ready_0=10, t_done_1=16, mx_ready_1=10, o_done=20, r_ready_0=10, r_ready_1=10),
    "act_gqa_x0": dict(mx_ready_0=1, t_done_1=2, mx_ready_1=1, o_done=2, r_ready_0=1, r_ready_1=1),
    "act_gqa_c0": dict(mx_ready_0=1, mx_ready_1=1, o_done=2, r_ready_0=1, r_ready_1=1),
    "act_gqa0": dict(mx_ready_0=10, t_done_1=16, mx_ready_1=10, o_done=20, r_ready_0=10, r_ready_1=10),
    "act_mla_x1": dict(mx_ready_0=1, t_done_1=2, mx_ready_1=1, o_done=2, r_ready_0=1, r_ready_1=1),
    "act_mla1": dict(stage_pe=2, stage_act=2, stage_dve=2, proj_done_0=2, proj_done_1=2, mx_ready_0=8, t_done_1=16, mx_ready_1=8, o_done=16, r_ready_0=8, r_ready_1=8),
    "act_gqa_x1": dict(mx_ready_0=1, t_done_1=2, mx_ready_1=1, o_done=2, r_ready_0=1, r_ready_1=1),
    "act_gqa1": dict(mx_ready_0=8, t_done_1=16, mx_ready_1=8, o_done=16, r_ready_0=8, r_ready_1=8),
    "act_index2": dict(index_done_0=1, relu_used_0=1, index_done_1=1, relu_used_1=1),
    "act_index3": dict(index_done_0=1, relu_used_0=1, index_done_1=1, relu_used_1=1),
    "act_index4": dict(index_done_0=1, relu_used_0=1, index_done_1=1, relu_used_1=1),
    "act_index5": dict(index_done_0=1, relu_used_0=1, index_done_1=1, relu_used_1=1),
    "act_index6": dict(index_done_0=1, relu_used_0=1, index_done_1=1, relu_used_1=1),
    "act_index7": dict(index_done_0=1, relu_used_0=1, index_done_1=1, relu_used_1=1),
    "act_gla": dict(stage_pe=4, stage_act=4, stage_dve=4, act_step=10, dve_to_act=5, pe_to_act=1, chunk_done=8),
    "act_dsa": dict(stage_pe=3, stage_act=3, stage_dve=3, mx_ready_0=8, t_done_1=8, mx_ready_1=8, o_done=16, r_ready_0=8, r_ready_1=8, pe_to_act=1),
    "act_mix": dict(gate_used=1),
    "act_up": dict(h_used_0=1, h_used_1=1, gate_convolved=1),
    "act_ple": dict(gate_used=1),
    "dve_taps0": dict(dve_step=1),
    "dve_mla_x0": dict(s_done_0=1, p_ready_0=1, t_done_0=2, s_done_1=1, t_done_2=2, p_ready_1=1, ot_done=1),
    "dve_mla_c0": dict(s_done_0=1, p_ready_0=1, t_done_0=2, s_done_1=1, p_ready_1=1, ot_done=1),
    "dve_mla0": dict(stage_pe=2, stage_act=2, stage_dve=2, dve_step=2, turned_0=1, turned_1=1, s_done_0=10, p_ready_0=10, t_done_0=20, s_done_1=10, t_done_2=16, p_ready_1=10, ot_done=10),
    "dve_gqa_x0": dict(s_done_0=1, p_ready_0=1, t_done_0=2, s_done_1=1, t_done_2=2, p_ready_1=1, ot_done=1),
    "dve_gqa_c0": dict(s_done_0=1, p_ready_0=1, t_done_0=2, s_done_1=1, p_ready_1=1, ot_done=1),
    "dve_gqa0": dict(s_done_0=10, p_ready_0=10, t_done_0=20, s_done_1=10, t_done_2=16, p_ready_1=10, ot_done=10),
    "dve_out0": dict(res_in_0=1, res_in_1=1),
    "dve_taps1": dict(dve_step=1),
    "dve_mla_x1": dict(s_done_0=1, p_ready_0=1, t_done_0=2, s_done_1=1, t_done_2=2, p_ready_1=1, ot_done=1),
    "dve_mla1": dict(stage_pe=2, stage_act=2, stage_dve=2, dve_step=2, turned_0=1, turned_1=1, s_done_0=8, p_ready_0=8, t_done_0=16, s_done_1=8, t_done_2=16, p_ready_1=8, ot_done=8),
    "dve_gqa_x1": dict(s_done_0=1, p_ready_0=1, t_done_0=2, s_done_1=1, t_done_2=2, p_ready_1=1, ot_done=1),
    "dve_gqa1": dict(s_done_0=8, p_ready_0=8, t_done_0=16, s_done_1=8, t_done_2=16, p_ready_1=8, ot_done=8),
    "dve_out1": dict(res_in_0=1, res_in_1=1),
    "dve_index2": dict(relu_used_0=1, relu_used_1=1, relu_ready_0=1, relu_ready_1=1),
    "dve_index3": dict(relu_used_0=1, relu_used_1=1, relu_ready_0=1, relu_ready_1=1),
    "dve_index4": dict(relu_used_0=1, relu_used_1=1, relu_ready_0=1, relu_ready_1=1),
    "dve_index5": dict(relu_used_0=1, relu_used_1=1, relu_ready_0=1, relu_ready_1=1),
    "dve_index6": dict(relu_used_0=1, relu_used_1=1, relu_ready_0=1, relu_ready_1=1),
    "dve_index7": dict(relu_used_0=1, relu_used_1=1, relu_ready_0=1, relu_ready_1=1),
    "dve_top2": dict(dve_step=2),
    "dve_top3": dict(dve_step=2),
    "dve_top4": dict(dve_step=2),
    "dve_top5": dict(dve_step=2),
    "dve_top6": dict(dve_step=2),
    "dve_top7": dict(dve_step=2),
    "dve_gla": dict(stage_pe=4, stage_act=4, stage_dve=4, dve_step=8, pe_to_dve=4, act_to_dve=5, update_done=7, state_ready=7, chunk_done=8, chunk_moved=8),
    "dve_dsa": dict(stage_pe=3, stage_act=3, stage_dve=3, s_done_0=8, p_ready_0=8, t_done_0=16, s_done_1=8, t_done_2=4, p_ready_1=8, ot_done=16),
    "dve_mix": dict(dve_step=1, gate_ready=1),
    "dve_up": dict(dve_step=4, h_used_0=1, h_ready_0=1, h_ready_1=1, silu_ready=1),
    "dve_ple": dict(dve_step=1, gate_ready=1),
}


def program(nc, io):
    hold = ExitStack()
    arena = hold.enter_context(nc.sbuf_tensor("arena", [P, ARENA], F32))
    psum = hold.enter_context(nc.psum_tensor("psum", [P, 4096], F32))

    def event(name, unit=1):
        return Event(name, hold.enter_context(nc.semaphore(name)), unit)

    def pair(name, unit=1):
        return [event(f"{name}_{s}", unit) for s in range(2)]

    def sb(at, n=1, p0=0, p1=P):
        if isinstance(at, int):
            return arena[p0:p1, at:at + n]
        return arena[p0:p1, bass.ds(at, n)]

    def ps(at, n, p0=0, p1=P):
        return psum[p0:p1, at:at + n]

    w_loaded, block_done = pair("w_loaded", 16), pair("block_done")
    psum_free = pair("psum_free")
    stage = {e: event(f"stage_{e}") for e in ("pe", "act", "dve")}
    consts_in, tables_in, params_in = (event(n, 16) for n in ("consts_in", "tables_in", "params_in"))
    attended = event("attended")
    x_in = event("x_in", 16)
    pe_step, act_step, dve_step = (event(f"{e}_step") for e in ("pe", "act", "dve"))
    waited = {e: event(f"waited_{e}") for e in ("pe", "act", "dve")}
    squares = pair("squares")
    squares_used = pair("squares_used")
    var_ready = event("var_ready")
    root_ready = event("root_ready")
    scaled = event("scaled")
    glu_gate = event("glu_gate")
    glu_used = event("glu_used")
    act_to_pe, act_to_dve, pe_to_act, pe_to_dve, dve_to_pe, dve_to_act = (
        event(n) for n in ("act_to_pe", "act_to_dve", "pe_to_act", "pe_to_dve", "dve_to_pe", "dve_to_act"))
    v_done = [event(f"v_done_{s}") for s in range(2)]
    v_moved = [event(f"v_moved_{s}") for s in range(2)]
    turned = pair("turned")
    turn_used = pair("turn_used")
    prep_moved = pair("prep_moved")
    hw_ready = pair("hw_ready")
    proj_done = pair("proj_done")
    q_ready = pair("q_ready")
    s_done = pair("s_done")
    mx_ready = pair("mx_ready")
    p_ready = pair("p_ready")
    r_ready = pair("r_ready")
    t_done = [event(f"t_done_{g}") for g in range(3)]
    t_moved = [event(f"t_moved_{g}") for g in range(3)]
    o_done = event("o_done")
    o_moved = event("o_moved")
    ot_done = event("ot_done")
    ot_used = event("ot_used")
    res_in = pair("res_in", 16)
    x_new = event("x_new")
    x_out = event("x_out", 16)
    index_done = pair("index_done")
    relu_ready = pair("relu_ready")
    relu_used = pair("relu_used")
    update_done = event("update_done")
    state_ready = event("state_ready")
    scaled_state = event("scaled_state")
    chunk_done = event("chunk_done")
    chunk_moved = event("chunk_moved")
    gate_ready = event("gate_ready")
    gate_used = event("gate_used")
    h_ready = pair("h_ready")
    h_used = pair("h_used")
    gate_convolved = event("gate_convolved")
    silu_ready = event("silu_ready")
    sparse_done = event("sparse_done")
    p_in = event("p_in", 16)
    finished = event("finished")
    stored = event("stored", 16)
    block = hold.enter_context(nc.Block())

    def con(name, n, p0=0, p1=P, off=0):
        return sb(CON_AT + CON[name] + off, n, p0, p1)

    def par(name, n=1, off=0, p0=0, p1=P):
        return sb(PAR_AT + (PA[name] if name in PA else PB[name]) + off, n, p0, p1)

    def barrier(t):
        t.alone()
        t.eng.drain().then_inc(stage[t.name].sem, 1)
        for e in stage.values():
            t.eng.wait_ge(e.sem, t.next(e))

    def uses(g, i=0, stride=0):
        return i * (stride // 2) + (g // 2 + 1) if stride else g // 2 + 1

    def pe_block(t, g, slot, rhs, cols, nk=KD):
        w = W_AT + (g % 2) * 1024
        t.eng.wait_ge(w_loaded[g % 2].sem, t.next(w_loaded[g % 2]))
        t.eng.wait_ge(psum_free[slot].sem, t.next(psum_free[slot]))
        for c0, n in cols:
            for k in range(nk):
                last = nc.tensor.matmul(ps(slot * SLOT + c0, n), lhsT=sb(w + k * P, P), rhs=rhs(k, c0, n),
                                        start=k == 0, stop=k == nk - 1)
        last.then_inc(block_done[g % 2].sem, 1)

    def pe_blocks(t, name, n, rhs, cols):
        g = BLOCKS[name]
        if n // 2:
            with t.loop(n // 2, name):
                for s in range(2):
                    pe_block(t, g + s, s, rhs, cols)
        if n % 2:
            pe_block(t, g + n - 1, 0, rhs, cols)

    def pe_stat(t, n_tiles, lhsT, at, cols):
        for k in range(n_tiles):
            s = t.tiles % 2
            t.tiles += 1
            t.eng.wait_ge(squares[s].sem, t.next(squares[s]))
            for c0, n in cols:
                last = nc.tensor.matmul(ps(at + c0, n), lhsT=lhsT, rhs=sb(TMP_AT + s * TC + c0, n),
                                        start=k == 0, stop=k == n_tiles - 1)
            last.then_inc(squares_used[s].sem, 1)

    def act_squares(t, src, n_tiles, width):
        for k in range(n_tiles):
            s = t.tiles % 2
            t.tiles += 1
            if t.tiles > 2:
                t.eng.wait_ge(squares_used[s].sem, t.next(squares_used[s]))
            nc.scalar.activation(sb(TMP_AT + s * TC, width), sb(src + k * TC, width), ACT.Square)\
                .then_inc(squares[s].sem, 1)

    def act_root(t, width):
        t.eng.wait_ge(var_ready.sem, t.next(var_ready))
        nc.scalar.activation(sb(STAT_AT, width), sb(STAT_AT, width), ACT.Ln).then_inc(act_step.sem, 1)
        t.eng.wait_ge(act_step.sem, t.next(act_step))
        nc.scalar.activation(sb(STAT_AT, width), sb(STAT_AT, width), ACT.Exp, scale=-0.5).then_inc(root_ready.sem, 1)

    def dve_rstd(t, n, eps, at, width, n_tiles):
        for _ in range(n_tiles):
            t.eng.wait_ge(squares_used[t.tiles % 2].sem, t.next(squares_used[t.tiles % 2]))
            t.tiles += 1
        nc.vector.tensor_scalar(sb(STAT_AT, width), ps(at, width), 1.0 / n, eps, ALU.mult, ALU.add)\
            .then_inc(var_ready.sem, 1)
        t.eng.wait_ge(root_ready.sem, t.next(root_ready))

    def layer_shapes(l):
        return TC if l < LAYERS - 1 else T

    def pe_mod(t):
        t.eng.wait_ge(act_to_pe.sem, t.next(act_to_pe))
        with t.loop(LAYERS * 12, "mod"):
            for s in range(2):
                t.eng.wait_ge(w_loaded[s].sem, t.next(w_loaded[s]))
                t.eng.wait_ge(psum_free[s].sem, t.next(psum_free[s]))
                for k in range(KD):
                    last = nc.tensor.matmul(ps(s * SLOT, 2), lhsT=sb(W_AT + s * 1024 + k * P, P),
                                            rhs=con("vec", 2, off=2 * k), start=k == 0, stop=k == KD - 1)
                last.then_inc(block_done[s].sem, 1)

    def act_mod(t):
        t.eng.wait_ge(consts_in.sem, t.next(consts_in))
        nc.scalar.activation(con("vec", 2 * KD), con("vec", 2 * KD), ACT.Silu).then_inc(act_to_pe.sem, 1)

    def dve_mod(t):
        t.eng.wait_ge(consts_in.sem, t.next(consts_in))
        with t.loop(LAYERS * 12, "mod") as i:
            for s in range(2):
                t.eng.wait_ge(block_done[(s) % 2].sem, uses(s, i, 2))
                nc.vector.tensor_scalar(sb(i * 4 + (MOD_AT + 2 * s), 2), ps(s * SLOT, 2),
                                        sb(i * 2 + (CON_AT + CON["b_mod"] + s), 1), None, ALU.add)\
                    .then_inc(psum_free[s].sem, 1)

    def gains(l):
        return MOD_AT + 48 * l

    def pe_norm(t, l):
        pe_stat(t, KD, con("ones", P), 0, chunks(TC))
        t.eng.wait_ge(var_ready.sem, t.next(var_ready))

    def act_norm(t, l):
        t.eng.wait_ge((x_out if l else x_in).sem, t.next(x_out if l else x_in, KD))
        t.eng.wait_ge(params_in.sem, t.next(params_in))
        act_squares(t, H_AT, KD, TC)
        act_root(t, TC)
        for k in range(KD):
            t.eng.wait_ge(scaled.sem, t.next(scaled))
            for v, (c0, n) in enumerate(((0, T), (T, C))):
                nc.scalar.activation(sb(H_AT + k * TC + c0, n), sb(H_AT + k * TC + c0, n), ACT.Identity,
                                     bias=sb(gains(l) + 2 * k + v), scale=sb(GAIN_AT + 2 * k + v))

    def dve_norm(t, l):
        t.eng.wait_ge((x_out if l else x_in).sem, t.next(x_out if l else x_in, KD))
        t.eng.wait_ge(params_in.sem, t.next(params_in))
        m = sb(gains(l) + 2 * KD, 2 * KD).rearrange("p (k v) -> p v k", v=2)
        for v in range(2):
            out = sb(GAIN_AT, 2 * KD).rearrange("p (k v) -> p v k", v=2)[:, v, :]
            nc.vector.scalar_tensor_tensor(out, m[:, v, :], 1.0, par("nw", KD), ALU.add, ALU.mult)
        dve_rstd(t, D, EPS, 0, TC, KD)
        for k in range(KD):
            nc.vector.tensor_tensor(sb(H_AT + k * TC, TC), sb(H_AT + k * TC, TC), sb(STAT_AT, TC), ALU.mult)\
                .then_inc(scaled.sem, 1)

    def pe_project(t, l):
        def h(k, c0, n):
            return sb(H_AT + k * TC + c0, n)
        cols = chunks(layer_shapes(l))
        pe_blocks(t, f"kv{l}", 4, h, chunks(TC))
        pe_blocks(t, f"q{l}", 5, h, cols)
        g = BLOCKS[f"conv{l}"]
        for j in range(4):
            pe_block(t, g + j, (j + 1) % 2, h, cols)
        g = BLOCKS[f"gate{l}"]
        with t.loop(4, f"gate{l}"):
            for s in range(2):
                pe_block(t, g + s, (s + 1) % 2, h, cols)

    def act_project(t, l):
        width = layer_shapes(l)
        g = BLOCKS[f"kv{l}"]
        with t.loop(2, f"kv{l}") as i:
            for s in range(2):
                t.eng.wait_ge(block_done[(g + s) % 2].sem, uses(g + s, i, 2))
                nc.scalar.activation(sb(i * (2 * TC) + (RAW_AT + s * TC), TC), ps(s * SLOT, TC), ACT.Copy)\
                    .then_inc(psum_free[s].sem, 1)
        g = BLOCKS[f"q{l}"]
        with t.loop(2, f"q{l}") as i:
            for s in range(2):
                t.eng.wait_ge(block_done[(g + s) % 2].sem, uses(g + s, i, 2))
                nc.scalar.activation(sb(i * (2 * TC) + (CQ_AT + s * TC), width), ps(s * SLOT, width), ACT.Copy)\
                    .then_inc(psum_free[s].sem, 1)
        t.eng.wait_ge(block_done[(g + 4) % 2].sem, uses(g + 4))
        nc.scalar.activation(sb(CQ_AT + 4 * TC, width), ps(0, width), ACT.Copy).then_inc(psum_free[0].sem, 1)
        g = BLOCKS[f"conv{l}"]
        for j in range(2):
            if j:
                t.eng.wait_ge(glu_used.sem, t.next(glu_used))
            t.eng.wait_ge(block_done[(g + 2 * j) % 2].sem, uses(g + 2 * j))
            nc.scalar.activation(sb(TMP_AT, width), ps(SLOT, width), ACT.Sigmoid).then_inc(psum_free[1].sem, 1)
            t.eng.drain().then_inc(glu_gate.sem, 1)
        g = BLOCKS[f"gate{l}"]
        nc.scalar.preload_act_table(ACT.Silu)
        with t.loop(4, f"gate{l}") as i:
            for s in range(2):
                t.eng.wait_ge(block_done[(g + s) % 2].sem, uses(g + s, i, 2))
                nc.scalar.activation(sb(i * (2 * TC) + (Y_AT + s * TC), width), ps(((s + 1) % 2) * SLOT, width), ACT.Silu)\
                    .then_inc(psum_free[(s + 1) % 2].sem, 1)
        t.eng.wait_ge(glu_used.sem, t.next(glu_used))

    def dve_project(t, l):
        segments = [(0, 0, T)] + ([(U_SEG, T, C)] if layer_shapes(l) > T else [])
        nc.vector.memset(sb(U_AT, 2 * U_LEN), 0.0).then_inc(dve_step.sem, 1)
        t.eng.wait_ge(dve_step.sem, t.next(dve_step))
        g = BLOCKS[f"conv{l}"]
        for j in range(2):
            t.eng.wait_ge(glu_gate.sem, t.next(glu_gate))
            t.eng.wait_ge(block_done[(g + 2 * j + 1) % 2].sem, uses(g + 2 * j + 1))
            for u0, c0, n in segments:
                last = nc.vector.tensor_tensor(sb(U_AT + j * U_LEN + u0 + PAD, n), ps(c0, n), sb(TMP_AT + c0, n), ALU.mult)
            last.then_inc(dve_step.sem, 1)
            t.eng.wait_ge(dve_step.sem, t.next(dve_step))
            t.alone()
            t.eng.drain().then_inc(psum_free[0].sem, 1)
            t.eng.drain().then_inc(glu_used.sem, 1)
        spans = [(j, U_AT + j * U_LEN + u0, ACC_AT + j * TC + c0, n) for j in range(2) for u0, c0, n in segments]
        for j, u, acc, n in spans:
            last = nc.vector.tensor_scalar(sb(acc, n), sb(u, n), par("dw", off=j), par("dwb", off=j), ALU.mult, ALU.add)
        last.then_inc(dve_step.sem, 1)
        t.eng.wait_ge(dve_step.sem, t.next(dve_step))
        with t.loop(CK - 1, f"taps{l}") as i:
            for j, u, acc, n in spans:
                last = nc.vector.scalar_tensor_tensor(sb(acc, n), sb(i + (u + 1), n), sb(i * 2 + (PAR_AT + PA["dw"] + 2 + j), 1),
                                                      sb(acc, n), ALU.mult, ALU.add)
            last.then_inc(dve_step.sem, 1)
            t.eng.wait_ge(dve_step.sem, t.next(dve_step))

    def pe_conv(t, l):
        cols = chunks(layer_shapes(l))
        for j in range(2):
            for c0, n in cols:
                last = nc.tensor.matmul(ps(c0, n), lhsT=con("ones", P), rhs=sb(ACC_AT + j * TC + c0, n),
                                        start=j == 0, stop=j == 1)
        last.then_inc(pe_to_dve.sem, 1)
        pe_stat(t, 2, con("ones", P), SLOT, cols)
        t.eng.wait_ge(var_ready.sem, t.next(var_ready))
        for m in range(2):
            for k in range(2):
                if m == 0:
                    t.eng.wait_ge(act_to_pe.sem, t.next(act_to_pe))
            for c0, n in cols:
                for k in range(2):
                    last = nc.tensor.matmul(ps(m * SLOT + c0, n), lhsT=par("pw", P, off=k * CC + m * P),
                                            rhs=sb(ACC_AT + k * TC + c0, n), start=k == 0, stop=k == 1)
            last.then_inc(pe_to_dve.sem, 1)

    def act_conv(t, l):
        width = layer_shapes(l)
        t.eng.wait_ge(dve_to_act.sem, t.next(dve_to_act))
        act_squares(t, ACC_AT, 2, width)
        act_root(t, width)
        for j in range(2):
            t.eng.wait_ge(dve_to_act.sem, t.next(dve_to_act))
            nc.scalar.activation(sb(ACC_AT + j * TC, width), sb(ACC_AT + j * TC, width), ACT.Silu,
                                 bias=par("lnb", off=j), scale=par("lnw", off=j)).then_inc(act_to_pe.sem, 1)

    def dve_conv(t, l):
        width = layer_shapes(l)
        t.eng.wait_ge(pe_to_dve.sem, t.next(pe_to_dve))
        nc.vector.tensor_scalar(sb(STAT_AT, width), ps(0, width), 1.0 / CC, None, ALU.mult).then_inc(dve_step.sem, 1)
        t.eng.wait_ge(dve_step.sem, t.next(dve_step))
        for j in range(2):
            last = nc.vector.tensor_tensor(sb(ACC_AT + j * TC, width), sb(ACC_AT + j * TC, width), sb(STAT_AT, width), ALU.subtract)
        last.then_inc(dve_step.sem, 1)
        t.eng.wait_ge(dve_step.sem, t.next(dve_step))
        t.alone()
        t.eng.drain().then_inc(dve_to_act.sem, 1)
        dve_rstd(t, CC, EPS, SLOT, width, 2)
        for j in range(2):
            nc.vector.tensor_tensor(sb(ACC_AT + j * TC, width), sb(ACC_AT + j * TC, width), sb(STAT_AT, width), ALU.mult)\
                .then_inc(dve_to_act.sem, 1)
        for m in range(2):
            t.eng.wait_ge(pe_to_dve.sem, t.next(pe_to_dve))
            y = Y_AT + (6 + m) * TC
            nc.vector.scalar_tensor_tensor(sb(y, width), ps(m * SLOT, width), par("pwb", off=m), sb(y, width), ALU.add, ALU.mult)

    def norm_groups(l):
        w = layer_shapes(l)
        return [(CKV_AT, 1, "ones", P, "kvn", TC), (CQ_AT, 2, "ones", 2 * P, "qn", w), (GK_AT, 1, "halves", GD, "gkn", TC)] + \
               [(GQ_AT + j * TC, 1, "halves", GD, "gqn", w) for j in range(3)]

    def pe_head_norms(t, l):
        for g, (_, tiles, ones, _, _, w) in enumerate(norm_groups(l)):
            if g >= 2:
                t.eng.wait_ge(var_ready.sem, t.next(var_ready))
            pe_stat(t, tiles, con(ones, P), (g % 2) * SLOT, chunks(w))
        t.eng.wait_ge(var_ready.sem, t.next(var_ready, 2))

    def act_head_norms(t, l):
        groups = norm_groups(l)
        for g, (at, tiles, _, _, _, w) in enumerate(groups):
            act_squares(t, at, tiles, w)
            if g:
                act_root(t, groups[g - 1][-1])
        act_root(t, groups[-1][-1])

    def dve_head_norms(t, l):
        for g, (at, tiles, _, n, gain, w) in enumerate(norm_groups(l)):
            dve_rstd(t, n, EPS, (g % 2) * SLOT, w, tiles)
            for j in range(tiles):
                last = nc.vector.scalar_tensor_tensor(sb(at + j * TC, w), sb(at + j * TC, w),
                                                      par(gain, off=j if tiles > 1 else 0), sb(STAT_AT, w), ALU.mult, ALU.mult)
            last.then_inc(dve_step.sem, 1)
            t.eng.wait_ge(dve_step.sem, t.next(dve_step))

    def pe_rope(t, l):
        for i, at in enumerate([KR_AT, GK_AT, GQ_AT, GQ_AT + TC, GQ_AT + 2 * TC]):
            rows = (64, 96) if i == 0 else (0, P)
            turn = con("turn_gqa", P) if i else con("turn_mla", MROPE, 64, 96)
            if i >= 2:
                t.eng.wait_ge(turn_used[i % 2].sem, t.next(turn_used[i % 2]))
            for c0, n in chunks(T):
                last = nc.tensor.matmul(ps((i % 2) * SLOT + c0, n, *rows), lhsT=turn, rhs=sb(at + c0, n, *rows), start=True, stop=True)
            last.then_inc(turned[i % 2].sem, 1)
            for j in range(2 * i, 2 * i + 2):
                if j >= 2:
                    t.eng.wait_ge(v_moved[j % 2].sem, t.next(v_moved[j % 2]))
                nc.tensor.matmul(ps(BANK6 + 512 * (j % 2), MH * MV), lhsT=sb(CKV_AT + j * P, P), rhs=par("uv", MH * MV),
                                 start=True, stop=True).then_inc(v_done[j % 2].sem, 1)
        for b, j0 in enumerate(range(0, 10, 4)):
            t.eng.wait_ge(v_moved[b % 2].sem, t.next(v_moved[b % 2]))
            for j in range(j0, min(j0 + 4, 10)):
                last = nc.tensor.transpose(ps(BANK6 + 512 * (b % 2) + (j - j0) * P, P), sb(GV_AT + j * P, P), con("ident", P))
            last.then_inc(v_done[b % 2].sem, 1)
        for s in range(2):
            t.eng.wait_ge(turn_used[s].sem, t.next(turn_used[s]))
            t.eng.wait_ge(v_moved[s].sem, t.next(v_moved[s]))

    def act_rope(t, l):
        for s in range(2):
            nc.scalar.activation(sb(KM_AT + s * TC + T, C, 64, 96), sb(KR_AT + T, C, 64, 96), ACT.Copy)
            nc.scalar.activation(sb(KG_AT + s * TC + T, C, 0, 64), sb(GK_AT + T, C, 64 * s, 64 * s + 64), ACT.Copy)
        for j in range(10):
            t.eng.wait_ge(v_done[j % 2].sem, t.next(v_done[j % 2]))
            nc.scalar.activation(sb(VM_AT + j * MH * MV, MH * MV), ps(BANK6 + 512 * (j % 2), MH * MV), ACT.Copy)\
                .then_inc(v_moved[j % 2].sem, 1)
        for b, j0 in enumerate(range(0, 10, 4)):
            n = min(4, 10 - j0) * P
            t.eng.wait_ge(v_done[b % 2].sem, t.next(v_done[b % 2]))
            nc.scalar.activation(sb(VG_AT + j0 * P, n), ps(BANK6 + 512 * (b % 2), n), ACT.Copy).then_inc(v_moved[b % 2].sem, 1)

    def dve_rope(t, l):
        for i, at in enumerate([KR_AT, GK_AT, GQ_AT, GQ_AT + TC, GQ_AT + 2 * TC]):
            r = (0, P) if i else (64, 96)
            table = TAB_AT + (TAB["gqa_cos"] if i else TAB["mla_cos"])
            t.eng.wait_ge(turned[i % 2].sem, t.next(turned[i % 2]))
            last = nc.vector.tensor_tensor(sb(at, T, *r), sb(at, T, *r), sb(table, T, *r), ALU.mult)
            nc.vector.tensor_tensor(sb(TMP_AT, T, *r), ps((i % 2) * SLOT, T, *r), sb(table + T, T, *r), ALU.mult)\
                .then_inc(turn_used[i % 2].sem, 1)
            t.eng.wait_ge(turn_used[i % 2].sem, t.next(turn_used[i % 2]))
            if i == 0:
                outs = [(sb(KM_AT + s * TC, T, 64, 96), 64, 96) for s in range(2)]
            elif i == 1:
                outs = [(sb(KG_AT + s * TC, T, 0, 64), 64 * s, 64 * s + 64) for s in range(2)]
            else:
                outs = [(sb(at, T), 0, P)]
            for out, p0, p1 in outs:
                last = nc.vector.tensor_tensor(out, sb(at, T, p0, p1), sb(TMP_AT, T, p0, p1), ALU.add)
            last.then_inc(dve_step.sem, 1)
            t.eng.wait_ge(dve_step.sem, t.next(dve_step))

    P_AT, PT_AT = TMP_AT, TMP_AT + 2 * TC
    MX_AT, SUM_AT, RS_AT = SMALL_AT, SMALL_AT + 2, SMALL_AT + 4
    O_PS, OT_PS = BANK7 + 256, BANK7 + 384

    def moves(n):
        groups = [(0, 0, min(n, 4)), (1, 4, min(n, 6) - 4 if n != 10 else 2), (2, 6, n - 6)]
        return [g for g in groups if g[2] > 0]

    def group_bank(g):
        return BANK7 if g == 1 else BANK6

    def pe_scores(t, s, rows, keys, nk):
        t.eng.wait_ge(q_ready[s].sem, t.next(q_ready[s]))
        if rows != P:
            t.alone()
        for c0, n in chunks(nk):
            last = nc.tensor.matmul(ps(s * SLOT + c0, n), lhsT=sb(QS_AT + s * P, P, 0, rows), rhs=keys(s, c0, n), start=True, stop=True)
        last.then_inc(s_done[s].sem, 1)

    def pe_out(t, s, nkt, values, dv):
        t.eng.wait_ge(p_ready[s].sem, t.next(p_ready[s]))
        for g, j0, n in moves(nkt):
            if g == 1:
                t.eng.wait_ge((o_moved if s else ot_used).sem, t.next(o_moved if s else ot_used))
            if g == 2:
                t.eng.wait_ge(t_moved[0].sem, t.next(t_moved[0]))
            for j in range(n):
                last = nc.tensor.transpose(ps(group_bank(g) + j * P, P), sb(P_AT + s * TC + (j0 + j) * P, P), con("ident", P))
            last.then_inc(t_done[g].sem, 1)
        if nkt <= 4:
            t.eng.wait_ge((o_moved if s else ot_used).sem, t.next(o_moved if s else ot_used))
        if nkt <= 6:
            t.eng.wait_ge(t_moved[0].sem, t.next(t_moved[0]))
        if nkt > 4:
            t.eng.wait_ge(t_moved[1].sem, t.next(t_moved[1]))
        for j in range(nkt):
            if j == 6:
                t.eng.wait_ge(t_moved[2].sem, t.next(t_moved[2]))
            last = nc.tensor.matmul(ps(O_PS, dv), lhsT=sb(PT_AT + s * TC + j * P, P), rhs=values(s, j), start=j == 0, stop=j == nkt - 1)
        last.then_inc(o_done.sem, 1)

    def pe_turn_out(t):
        t.eng.wait_ge(o_moved.sem, t.next(o_moved))
        nc.tensor.transpose(ps(OT_PS, P), sb(OT_AT, P), con("ident", P)).then_inc(ot_done.sem, 1)

    def pe_attend(t, name, tiles, rows, keys, nkt, values):
        pe_scores(t, 0, rows, keys, nkt * P)

        def unit(more):
            pe_scores(t, 1, rows, keys, nkt * P)
            pe_out(t, 0, nkt, values, 64)
            if more:
                pe_scores(t, 0, rows, keys, nkt * P)
            pe_out(t, 1, nkt, values, 64)
            pe_turn_out(t)
        with t.loop(tiles - 1, name):
            unit(True)
        unit(False)

    def act_query(t, s, rows, query, tile, scale):
        nc.scalar.activation(sb(QS_AT + s * P, P, 0, rows), query(s, tile), ACT.Copy, scale=scale).then_inc(q_ready[s].sem, 1)

    def act_exp(t, s, nk):
        t.eng.wait_ge(mx_ready[s].sem, t.next(mx_ready[s]))
        nc.scalar.activation(sb(P_AT + s * TC, nk), ps(s * SLOT, nk), ACT.Exp, bias=sb(MX_AT + s),
                             accum_out=sb(SUM_AT + s)).then_inc(p_ready[s].sem, 1)

    def act_move(t, s, g, j0, n):
        t.eng.wait_ge(t_done[g].sem, t.next(t_done[g]))
        nc.scalar.activation(sb(PT_AT + s * TC + j0 * P, n * P), ps(group_bank(g), n * P), ACT.Copy).then_inc(t_moved[g].sem, 1)

    def act_out(t, s, dv=64, at=0):
        t.eng.wait_ge(o_done.sem, t.next(o_done))
        t.eng.wait_ge(r_ready[s].sem, t.next(r_ready[s]))
        nc.scalar.activation(sb(OT_AT + at, dv), ps(O_PS, dv), ACT.Copy, scale=sb(RS_AT + s)).then_inc(o_moved.sem, 1)

    def act_attend(t, name, tiles, rows, query, nkt, scale, tile0=0):
        act_query(t, 0, rows, query, tile0, scale)
        act_query(t, 1, rows, query, tile0, scale)
        act_exp(t, 0, nkt * P)

        def unit(tile, more):
            groups = moves(nkt)
            if more:
                act_query(t, 0, rows, query, tile + 1, scale)
            if len(groups) > 1:
                act_move(t, 0, *groups[1])
            act_exp(t, 1, nkt * P)
            act_out(t, 0)
            if more:
                act_query(t, 1, rows, query, tile + 1, scale)
            if len(groups) > 1:
                act_move(t, 1, *groups[1])
            if more:
                act_exp(t, 0, nkt * P)
            act_out(t, 1, at=64)
        with t.loop(tiles - 1, name) as i:
            unit(i + tile0, True)
        unit(tile0 + tiles - 1, False)

    def dve_max(t, s, nk):
        t.eng.wait_ge(s_done[s].sem, t.next(s_done[s]))
        nc.vector.tensor_reduce(sb(MX_AT + s), ps(s * SLOT, nk), AX.X, ALU.max, negate=True).then_inc(mx_ready[s].sem, 1)

    def dve_recip(t, s):
        t.eng.wait_ge(p_ready[s].sem, t.next(p_ready[s]))
        nc.vector.reciprocal(sb(RS_AT + s), sb(SUM_AT + s)).then_inc(r_ready[s].sem, 1)

    def dve_move(t, s, g, j0, n):
        t.eng.wait_ge(t_done[g].sem, t.next(t_done[g]))
        nc.vector.tensor_copy(sb(PT_AT + s * TC + j0 * P, n * P), ps(group_bank(g), n * P)).then_inc(t_moved[g].sem, 1)

    def dve_attend(t, name, tiles, nkt, mixed, tile0=0):
        groups = moves(nkt)
        dve_max(t, 0, nkt * P)

        def unit(tile, more):
            dve_recip(t, 0)
            dve_move(t, 0, *groups[0])
            dve_max(t, 1, nkt * P)
            if len(groups) > 2:
                dve_move(t, 0, *groups[2])
            dve_recip(t, 1)
            dve_move(t, 1, *groups[0])
            if more:
                dve_max(t, 0, nkt * P)
            if len(groups) > 2:
                dve_move(t, 1, *groups[2])
            t.eng.wait_ge(ot_done.sem, t.next(ot_done))
            y = mixed(tile)
            nc.vector.tensor_tensor(y, y, ps(OT_PS, P), ALU.mult).then_inc(ot_used.sem, 1)
        with t.loop(tiles - 1, name) as i:
            unit(i + tile0, True)
        unit(tile0 + tiles - 1, False)

    def pe_mla(t, l):
        w = chunks(layer_shapes(l))
        with t.loop(MH // 2, f"mla{l}") as p:
            for s in range(2):
                t.eng.wait_ge(hw_ready[s].sem, t.next(hw_ready[s]))
                for c0, n in chunks(TC):
                    last = nc.tensor.matmul(ps(s * SLOT + c0, n, 0, MNOPE), lhsT=sb(HW_AT + s * 256 + 2 * MQ, MNOPE),
                                            rhs=sb(CKV_AT + c0, n), start=True, stop=True)
                last.then_inc(proj_done[s].sem, 1)
            for s in range(2):
                t.eng.wait_ge(prep_moved[s].sem, t.next(prep_moved[s]))
                for c0, n in w:
                    for k in range(2):
                        last = nc.tensor.matmul(ps(s * SLOT + c0, n, 0, MQ), lhsT=sb(HW_AT + s * 256 + k * MQ, MQ),
                                                rhs=sb(CQ_AT + k * TC + c0, n), start=k == 0, stop=k == 1)
                last.then_inc(proj_done[s].sem, 1)
            for s in range(2):
                t.eng.wait_ge(prep_moved[s].sem, t.next(prep_moved[s]))
                t.alone()
                for c0, n in chunks(T):
                    last = nc.tensor.matmul(ps(s * SLOT + c0, n, 64, 96), lhsT=con("turn_mla", MROPE, 64, 96),
                                            rhs=sb(QM_AT + s * TC + c0, n, 64, 96), start=True, stop=True)
                last.then_inc(turned[s].sem, 1)
            barrier(t)

            def values(s, j):
                return sb(p * P + (VM_AT + j * MH * MV + 64 * s), MV)
            pe_attend(t, f"mla_x{l}", QT, MQ, lambda s, c0, n: sb(KM_AT + s * TC + c0, n, 0, MQ), TC // P, values)
            if l == 0:
                pe_attend(t, f"mla_c{l}", 2, MQ, lambda s, c0, n: sb(KM_AT + s * TC + T + c0, n, 0, MQ), C // P,
                          lambda s, j: values(s, j + QT))
            barrier(t)

    def act_mla(t, l):
        w = layer_shapes(l)
        with t.loop(MH // 2, f"mla{l}") as p:
            for s in range(2):
                nc.scalar.activation(sb(HW_AT + s * 256, 256), sb(p * 512 + (PAR_AT + PA["uqk"] + s * 256), 256), ACT.Copy)\
                    .then_inc(hw_ready[s].sem, 1)
            for s in range(2):
                t.eng.wait_ge(proj_done[s].sem, t.next(proj_done[s]))
                nc.scalar.activation(sb(KM_AT + s * TC, TC, 0, MNOPE), ps(s * SLOT, TC, 0, MNOPE), ACT.Copy)\
                    .then_inc(prep_moved[s].sem, 1)
            for s in range(2):
                t.eng.wait_ge(proj_done[s].sem, t.next(proj_done[s]))
                nc.scalar.activation(sb(QM_AT + s * TC, w, 0, MQ), ps(s * SLOT, w, 0, MQ), ACT.Copy)\
                    .then_inc(prep_moved[s].sem, 1)
            barrier(t)

            def query(s, tile):
                return sb(tile * P + (QM_AT + s * TC), P, 0, MQ)
            act_attend(t, f"mla_x{l}", QT, MQ, query, TC // P, MQ ** -0.5)
            if l == 0:
                act_attend(t, f"mla_c{l}", 2, MQ, query, C // P, MQ ** -0.5, tile0=QT)
            barrier(t)

    def dve_mla(t, l):
        with t.loop(MH // 2, f"mla{l}") as p:
            for s in range(2):
                t.eng.wait_ge(turned[s].sem, t.next(turned[s]))
                q = sb(QM_AT + s * TC, T, 64, 96)
                last = nc.vector.tensor_tensor(q, q, sb(TAB_AT + TAB["mla_cos"], T, 64, 96), ALU.mult)
                nc.vector.tensor_tensor(sb(TMP_AT + s * TC, T, 64, 96), ps(s * SLOT, T, 64, 96),
                                        sb(TAB_AT + TAB["mla_sin"], T, 64, 96), ALU.mult).then_inc(dve_step.sem, 1)
                t.eng.wait_ge(dve_step.sem, t.next(dve_step))
                nc.vector.tensor_tensor(q, q, sb(TMP_AT + s * TC, T, 64, 96), ALU.add)
            barrier(t)

            def mixed(tile):
                return sb(p * TC + tile * P + Y_AT, P)
            dve_attend(t, f"mla_x{l}", QT, TC // P, mixed)
            if l == 0:
                dve_attend(t, f"mla_c{l}", 2, C // P, mixed, tile0=QT)
            barrier(t)

    def pe_gqa(t, l):
        with t.loop(GH // 2, f"gqa{l}"):
            def values(s, j):
                return sb(VG_AT + j * P + 64 * s, GD)
            pe_attend(t, f"gqa_x{l}", QT, GD, lambda s, c0, n: sb(KG_AT + s * TC + c0, n, 0, GD), TC // P, values)
            if l == 0:
                pe_attend(t, f"gqa_c{l}", 2, GD, lambda s, c0, n: sb(KG_AT + s * TC + T + c0, n, 0, GD), C // P,
                          lambda s, j: values(s, j + QT))

    def act_gqa(t, l):
        with t.loop(GH // 2, f"gqa{l}") as p:
            def query(s, tile):
                return sb(p * TC + tile * P + GQ_AT, P, 64 * s, 64 * s + 64)
            act_attend(t, f"gqa_x{l}", QT, GD, query, TC // P, GD ** -0.5)
            if l == 0:
                act_attend(t, f"gqa_c{l}", 2, GD, query, C // P, GD ** -0.5, tile0=QT)

    def dve_gqa(t, l):
        with t.loop(GH // 2, f"gqa{l}") as p:
            def mixed(tile):
                return sb(p * TC + tile * P + (Y_AT + 3 * TC), P)
            dve_attend(t, f"gqa_x{l}", QT, TC // P, mixed)
            if l == 0:
                dve_attend(t, f"gqa_c{l}", 2, C // P, mixed, tile0=QT)

    def pe_outproj(t, l):
        pe_blocks(t, f"out{l}", 8, lambda k, c0, n: sb(Y_AT + k * TC + c0, n), chunks(layer_shapes(l)))

    def dve_outproj(t, l):
        g = BLOCKS[f"out{l}"]
        segments = [(0, T, 0), (T, C, 1)][:2 if layer_shapes(l) > T else 1]
        gate = gains(l) + 4 * KD
        with t.loop(KD // 2, f"out{l}") as i:
            for s in range(2):
                t.eng.wait_ge(res_in[s].sem, t.next(res_in[s]))
                t.eng.wait_ge(block_done[(g + s) % 2].sem, uses(g + s, i, 2))
                for c0, n, v in segments:
                    nc.vector.scalar_tensor_tensor(sb(i * (2 * TC) + (H_AT + s * TC + c0), n), ps(s * SLOT + c0, n),
                                                   sb(i * 4 + (gate + 2 * s + v)), sb(TMP_AT + s * TC + c0, n), ALU.mult, ALU.add)
                t.eng.drain().then_inc(psum_free[s].sem, 1)
                t.eng.drain().then_inc(x_new.sem, 1)

    def pool_layer(t, l):
        source = io["x0"] if l == 0 else io["x_mid"]
        t.eng.wait_ge(attended.sem, t.next(attended))
        t.eng.dma_start(sb(PAR_AT, NPA if l + 1 < LAYERS else NPB), io["par_a"][l + 1] if l + 1 < LAYERS else io["par_b"])\
            .then_inc(params_in.sem, 16)
        for m in range(KD + 2):
            if m >= 2:
                t.eng.wait_ge(x_new.sem, t.next(x_new))
                if l == 0:
                    t.eng.dma_start(io["x_mid"][:, (m - 2) * TC:(m - 1) * TC], sb(H_AT + (m - 2) * TC, TC)).then_inc(x_out.sem, 16)
            if m < KD:
                w = layer_shapes(l)
                t.eng.dma_start(sb(TMP_AT + (m % 2) * TC, w), source[:, m * TC:m * TC + w]).then_inc(res_in[m % 2].sem, 16)

    def x_tile(k, c0=0, n=T):
        return sb(X_AT + k * TC + c0, n)

    def x_rhs(k, c0, n):
        return sb(X_AT + k * TC + c0, n)

    def pe_final(t):
        pe_stat(t, KD, con("ones", P), 0, chunks(T))
        t.eng.wait_ge(var_ready.sem, t.next(var_ready))

    def act_final(t):
        t.eng.wait_ge(params_in.sem, t.next(params_in))
        act_squares(t, X_AT, KD, T)
        act_root(t, T)

    def dve_final(t):
        t.eng.wait_ge(params_in.sem, t.next(params_in))
        dve_rstd(t, D, EPS, 0, T, KD)
        for k in range(KD):
            nc.vector.scalar_tensor_tensor(x_tile(k), x_tile(k), con("final_w", 1, off=k), sb(STAT_AT, T), ALU.mult, ALU.mult)

    def act_index_proj(t):
        g = BLOCKS["index"]
        with t.loop(2, "iq") as i:
            for s in range(2):
                t.eng.wait_ge(block_done[(g + s) % 2].sem, uses(g + s, i, 2))
                nc.scalar.activation(sb(i * (4 * T) + (MIX_AT + 2 * s * T), T, 0, 64), ps(s * SLOT, T, 0, 64), ACT.Copy)
                nc.scalar.activation(sb(i * (4 * T) + (MIX_AT + (2 * s + 1) * T), T, 0, 64), ps(s * SLOT, T, 64, P), ACT.Copy)\
                    .then_inc(psum_free[s].sem, 1)
        for s, at in enumerate((CL_AT, MISC_AT)):
            t.eng.wait_ge(block_done[(g + 4 + s) % 2].sem, uses(g + 4 + s))
            nc.scalar.activation(sb(at, T), ps(s * SLOT, T), ACT.Copy).then_inc(psum_free[s].sem, 1)

    def pe_latents(t):
        pe_stat(t, 1, con("ones", P), 0, chunks(T))
        t.eng.wait_ge(var_ready.sem, t.next(var_ready))
        for j in range(QT):
            last = nc.tensor.transpose(ps(SLOT + j * P, P), sb(MISC_AT + j * P, P), con("ident", P))
        last.then_inc(pe_to_act.sem, 1)
        t.eng.wait_ge(dve_to_pe.sem, t.next(dve_to_pe))
        for j in range(QT):
            last = nc.tensor.transpose(ps(j * P, P), sb(CL_AT + j * P, P), con("ident", P))
        last.then_inc(pe_to_act.sem, 1)

    def act_latents(t):
        act_squares(t, CL_AT, 1, T)
        act_root(t, T)
        t.eng.wait_ge(pe_to_act.sem, t.next(pe_to_act))
        nc.scalar.activation(sb(IW_AT, QT * IH).rearrange("p (j h) -> p j h", h=IH),
                             ps(SLOT, T).rearrange("p (j f) -> p j f", f=P)[:, :, 96:96 + IH], ACT.Copy,
                             scale=IH ** -0.5 * ID_ ** -0.5)
        t.eng.wait_ge(pe_to_act.sem, t.next(pe_to_act))
        nc.scalar.activation(sb(CLT_AT, T), ps(0, T), ACT.Copy)

    def dve_latents(t):
        nc.vector.memset(sb(MASK_AT, MISC_AT - MASK_AT), 0.0).then_inc(dve_step.sem, 1)
        t.eng.wait_ge(dve_step.sem, t.next(dve_step))
        dve_rstd(t, DL, LN_EPS, 0, T, 1)
        nc.vector.scalar_tensor_tensor(sb(CL_AT, T), sb(CL_AT, T), par("ckv_n"), sb(STAT_AT, T), ALU.mult, ALU.mult)\
            .then_inc(dve_to_pe.sem, 1)

    INDEX_TILES = range(TOPK // P, QT)

    def pe_scores_index(t):
        for j in INDEX_TILES:
            with t.loop(IH // 2, f"index{j}"):
                for s in range(2):
                    t.eng.wait_ge(q_ready[s].sem, t.next(q_ready[s]))
                    t.alone()
                    for c0, n in chunks((j + 1) * P):
                        last = nc.tensor.matmul(ps(s * SLOT + c0, n), lhsT=sb(QS_AT + s * P, P, 0, ID_), rhs=sb(MISC_AT + c0, n, 0, ID_),
                                                start=True, stop=True)
                    last.then_inc(index_done[s].sem, 1)

    def act_scores_index(t):
        for j in INDEX_TILES:
            with t.loop(IH // 2, f"index{j}") as i:
                for s in range(2):
                    nc.scalar.activation(sb(QS_AT + s * P, P, 0, ID_), sb(i * (2 * T) + (MIX_AT + s * T + j * P), P, 0, ID_), ACT.Copy)\
                        .then_inc(q_ready[s].sem, 1)
                for s in range(2):
                    t.eng.wait_ge(index_done[s].sem, t.next(index_done[s]))
                    t.eng.wait_ge(relu_used[s].sem, t.next(relu_used[s]))
                    nc.scalar.activation(sb(TMP_AT + s * TC, (j + 1) * P), ps(s * SLOT, (j + 1) * P), ACT.Relu)\
                        .then_inc(relu_ready[s].sem, 1)

    def dve_scores_index(t):
        for s in range(2):
            nc.vector.memset(sb(SMALL_AT + 8 + s), 0.0).then_inc(relu_used[s].sem, 1)
            t.eng.wait_ge(relu_used[s].sem, t.next(relu_used[s]))
        for j in INDEX_TILES:
            w = (j + 1) * P
            with t.loop(IH // 2, f"index{j}") as i:
                for s in range(2):
                    t.eng.wait_ge(relu_ready[s].sem, t.next(relu_ready[s]))
                    ins = nc.vector.scalar_tensor_tensor(sb(mask_at(j), w), sb(TMP_AT + s * TC, w), sb(i * 2 + (IW_AT + j * IH + s)),
                                                         sb(mask_at(j), w), ALU.mult, ALU.add)
                    ins.then_inc(relu_used[s].sem, 1)
                    t.eng.wait_ge(relu_used[s].sem, t.next(relu_used[s]))
                    t.alone()
        for j in range(QT):
            m = sb(mask_at(j) + j * P, P)
            nc.vector.tensor_tensor(m, m, con("later", P), ALU.subtract if j in INDEX_TILES else ALU.add)

    def pe_gates(t):
        pe_blocks(t, "gates_a", KD, x_rhs, chunks(T))
        pe_blocks(t, "gr", KD, x_rhs, chunks(T))

    def act_gates(t):
        for name, at, func in (("gates_a", MIX_AT, ACT.Sigmoid), ("gr", GR_AT, ACT.Silu)):
            nc.scalar.preload_act_table(func)
            with t.loop(KD // 2, name) as i:
                for s in range(2):
                    t.eng.wait_ge(block_done[(BLOCKS[name] + s) % 2].sem, uses(BLOCKS[name] + s, i, 2))
                    nc.scalar.activation(sb(i * (2 * T) + (at + s * T), T), ps(s * SLOT, T), func).then_inc(psum_free[s].sem, 1)

    def dve_select(t):
        work, top, equal, upto = TMP_AT, SMALL_AT + 16, TMP_AT + TC, TMP_AT + 2 * TC
        count = SMALL_AT + 24
        for j in INDEX_TILES:
            w, m = (j + 1) * P, mask_at(j)
            nc.vector.tensor_copy(sb(work, w), sb(m, w)).then_inc(dve_step.sem, 1)
            t.eng.wait_ge(dve_step.sem, t.next(dve_step))
            t.alone()
            nc.vector.max(out=sb(top, 8), in_=sb(work, w)).then_inc(dve_step.sem, 1)
            t.eng.wait_ge(dve_step.sem, t.next(dve_step))
            with t.loop(TOPK // 8 - 1, f"top{j}"):
                t.alone()
                nc.vector.match_replace(out=sb(work, w), in_to_replace=sb(top, 8), in_values=sb(work, w), imm_value=LOW).then_inc(dve_step.sem, 1)
                t.eng.wait_ge(dve_step.sem, t.next(dve_step))
                t.alone()
                nc.vector.max(out=sb(top, 8), in_=sb(work, w)).then_inc(dve_step.sem, 1)
                t.eng.wait_ge(dve_step.sem, t.next(dve_step))
            nc.vector.tensor_scalar(sb(equal, w), sb(m, w), sb(top + 7), None, ALU.is_equal)
            nc.vector.tensor_scalar(sb(work, w), sb(m, w), sb(top + 7), None, ALU.is_gt, ALU.add, accum_out=sb(count)).then_inc(dve_step.sem, 1)
            t.eng.wait_ge(dve_step.sem, t.next(dve_step))
            nc.vector.tensor_scalar(sb(count), sb(count), -1.0, float(TOPK), ALU.mult, ALU.add).then_inc(dve_step.sem, 1)
            t.eng.wait_ge(dve_step.sem, t.next(dve_step))
            nc.vector.tensor_tensor_scan(sb(upto, w), sb(equal, w), sb(equal, w), 0.0, ALU.add, ALU.max).then_inc(dve_step.sem, 1)
            t.eng.wait_ge(dve_step.sem, t.next(dve_step))
            nc.vector.scalar_tensor_tensor(sb(upto, w), sb(upto, w), sb(count), sb(equal, w), ALU.is_le, ALU.mult).then_inc(dve_step.sem, 1)
            t.eng.wait_ge(dve_step.sem, t.next(dve_step))
            nc.vector.tensor_tensor(sb(work, w), sb(work, w), sb(upto, w), ALU.add).then_inc(dve_step.sem, 1)
            t.eng.wait_ge(dve_step.sem, t.next(dve_step))
            nc.vector.tensor_scalar(sb(m, w), sb(work, w), NEG, -NEG, ALU.mult, ALU.add).then_inc(dve_step.sem, 1)
            t.eng.wait_ge(dve_step.sem, t.next(dve_step))

    def value_tile(c, off=0, n=GDV):
        return sb(GAP_AT + c * TC + off, n)

    def pe_gla(t):
        g = BLOCKS["gla"]
        with t.loop(GLH, "gla"):
            pe_block(t, g, 0, x_rhs, chunks(T))
            pe_block(t, g + 1, 1, x_rhs, chunks(T))
            t.eng.wait_ge(act_to_pe.sem, t.next(act_to_pe))
            for c0, n in chunks(T):
                last = nc.tensor.matmul(ps(BANK6 + c0, n), lhsT=sb(HW_AT, P, 64, 64 + GRANK), rhs=sb(MISC_AT + c0, n, 64, 64 + GRANK),
                                        start=True, stop=True)
            last.then_inc(pe_to_dve.sem, 1)
            for s in range(2):
                t.eng.wait_ge(w_loaded[s].sem, t.next(w_loaded[s]))
                t.eng.wait_ge(psum_free[s].sem, t.next(psum_free[s]))
                for c in range(QT):
                    for k in range(KD):
                        last = nc.tensor.matmul(ps(s * SLOT + c * P, P), lhsT=x_tile(k, c * P, P), rhs=sb(W_AT + s * 1024 + k * P, P),
                                                start=k == 0, stop=k == KD - 1)
                last.then_inc(block_done[s].sem, 1)
            barrier(t)
            for c in range(QT):
                last = nc.tensor.transpose(ps(c * P, P), sb(GLA_KS + c * P, P), con("ident", P))
            last.then_inc(pe_to_act.sem, 1)
            for c in range(QT):
                last = nc.tensor.matmul(ps(SLOT + c * P, P), lhsT=sb(GLA_K + c * P, P), rhs=sb(GLA_Q + c * P, P), start=True, stop=True)
            last.then_inc(pe_to_dve.sem, 1)
            barrier(t)
            for c in range(QT):
                if c < QT - 1:
                    if c >= 2:
                        t.eng.wait_ge(state_ready.sem, t.next(state_ready))
                    nc.tensor.matmul(ps((c % 2) * 512, GDV), lhsT=sb(GLA_L + c * P, P), rhs=value_tile(c), start=True, stop=True)\
                        .then_inc(update_done.sem, 1)
                if c >= 2:
                    t.eng.wait_ge(chunk_moved.sem, t.next(chunk_moved))
                last = nc.tensor.matmul(ps(SLOT + (c % 2) * 512, GDV), lhsT=sb(GLA_B + c * P, P), rhs=value_tile(c), start=True, stop=c == 0)
                if c:
                    t.eng.wait_ge(scaled_state.sem, t.next(scaled_state))
                    last = nc.tensor.matmul(ps(SLOT + (c % 2) * 512, GDV), lhsT=sb(GLA_Q + c * P, P), rhs=sb(GLA_SM, GDV), start=False, stop=True)
                last.then_inc(chunk_done.sem, 1)
            t.eng.wait_ge(state_ready.sem, t.next(state_ready, 2))
            t.eng.wait_ge(chunk_moved.sem, t.next(chunk_moved, 2))
            barrier(t)
            for half in range(2):
                for c in range(QT):
                    last = nc.tensor.transpose(ps(half * SLOT + c * P, P), sb(GLA_O + c * GDV + half * P, P), con("ident", P))
                last.then_inc(pe_to_dve.sem, 1)
            barrier(t)

    def act_gla(t):
        g = BLOCKS["gla"]
        with t.loop(GLH, "gla") as h:
            nc.scalar.activation(sb(HW_AT, P, 64, 64 + GRANK), sb(h * P + (PAR_AT + PB["gate_up"]), P, 64, 64 + GRANK), ACT.Copy)\
                .then_inc(act_to_pe.sem, 1)
            for s, (at, scale) in enumerate(((GLA_Q, GDK ** -0.5), (GLA_K, 1.0))):
                t.eng.wait_ge(block_done[(g + s) % 2].sem, uses(g + s, h, 4))
                nc.scalar.activation(sb(at, T), ps(s * SLOT, T), ACT.Copy, scale=scale).then_inc(psum_free[s].sem, 1)
            t.eng.wait_ge(dve_to_act.sem, t.next(dve_to_act))
            nc.scalar.activation(sb(GLA_L, T), sb(GLA_E, T), ACT.Abs).then_inc(act_step.sem, 1)
            t.eng.wait_ge(act_step.sem, t.next(act_step))
            nc.scalar.activation(sb(GLA_L, T), sb(GLA_L, T), ACT.Exp, scale=-1.0).then_inc(act_step.sem, 1)
            t.eng.wait_ge(act_step.sem, t.next(act_step))
            nc.scalar.activation(sb(GLA_L, T), sb(GLA_L, T), ACT.Ln, bias=1.0).then_inc(act_to_dve.sem, 1)
            for s in range(2):
                t.eng.wait_ge(block_done[(g + 2 + s) % 2].sem, uses(g + 2 + s, h, 4))
                out = sb(GAP_AT, QT * TC).rearrange("p (c n) -> p c n", n=TC)[:, :, s * P:(s + 1) * P]
                nc.scalar.activation(out, ps(s * SLOT, T).rearrange("p (c n) -> p c n", n=P), ACT.Copy).then_inc(psum_free[s].sem, 1)
            t.eng.wait_ge(dve_to_act.sem, t.next(dve_to_act))
            nc.scalar.activation(sb(GLA_SMALL + 8, QT), sb(GLA_SMALL + 8, QT), ACT.Exp)
            nc.scalar.activation(sb(GLA_SMALL + 24, QT), sb(GLA_SMALL + 16, QT), ACT.Exp)
            for i, (sign, bias) in enumerate(((-1.0, 16), (-1.0, 32), (1.0, 0))):
                if i:
                    t.eng.wait_ge(dve_to_act.sem, t.next(dve_to_act))
                for c in range(QT):
                    last = nc.scalar.activation(sb(GLA_E + c * P, P), sb(GLA_B + c * P, P), ACT.Exp, scale=sign / GTEMP,
                                                bias=sb(GLA_SMALL + bias + c))
                last.then_inc(act_to_dve.sem, 1)
            barrier(t)
            t.eng.wait_ge(pe_to_act.sem, t.next(pe_to_act))
            nc.scalar.activation(sb(GLA_L, T), ps(0, T), ACT.Copy)
            barrier(t)
            for c in range(QT):
                t.eng.wait_ge(chunk_done.sem, t.next(chunk_done))
                nc.scalar.activation(sb(GLA_E, GDV), ps(SLOT + (c % 2) * 512, GDV), ACT.Square, accum_out=sb(GLA_SMALL + 40 + c)).then_inc(act_step.sem, 1)
                t.eng.wait_ge(act_step.sem, t.next(act_step))
                nc.scalar.activation(sb(GLA_O + c * GDV, GDV), ps(SLOT + (c % 2) * 512, GDV), ACT.Copy).then_inc(chunk_moved.sem, 1)
            t.eng.wait_ge(dve_to_act.sem, t.next(dve_to_act))
            nc.scalar.activation(sb(GLA_SMALL + 40, QT), sb(GLA_SMALL + 40, QT), ACT.Sqrt).then_inc(act_to_dve.sem, 1)
            barrier(t)
            barrier(t)

    def dve_gla(t):
        with t.loop(GLH, "gla") as h:
            t.eng.wait_ge(pe_to_dve.sem, t.next(pe_to_dve))
            nc.vector.tensor_scalar(sb(GLA_E, T), ps(BANK6, T), sb(h + (PAR_AT + PB["b_gate"])), None, ALU.add).then_inc(dve_step.sem, 1)
            t.eng.wait_ge(dve_step.sem, t.next(dve_step))
            t.alone()
            t.eng.drain().then_inc(dve_to_act.sem, 1)
            t.eng.wait_ge(act_to_dve.sem, t.next(act_to_dve))
            nc.vector.scalar_tensor_tensor(sb(GLA_L, T), sb(GLA_E, T), 0.0, sb(GLA_L, T), ALU.min, ALU.subtract).then_inc(dve_step.sem, 1)
            t.eng.wait_ge(dve_step.sem, t.next(dve_step))
            for c in range(QT):
                last = nc.vector.tensor_tensor_scan(sb(GLA_B + c * P, P), sb(GLA_L + c * P, P), sb(GLA_L + c * P, P), 0.0, ALU.add, ALU.min)
            last.then_inc(dve_step.sem, 1)
            t.eng.wait_ge(dve_step.sem, t.next(dve_step))
            b = sb(GLA_B, T).rearrange("p (c n) -> p c n", n=P)
            small = [sb(GLA_SMALL + 8 * i, QT).rearrange("p (c n) -> p c n", n=1) for i in range(5)]
            middle, end = b[:, :, P // 2 - 1:P // 2], b[:, :, P - 1:P]
            nc.vector.tensor_scalar(small[0], middle, -1.0 / GTEMP, None, ALU.mult)
            nc.vector.tensor_scalar(small[1], middle, 1.0 / GTEMP, None, ALU.mult)
            nc.vector.tensor_scalar(small[4], middle, 1.0 / GTEMP, None, ALU.mult)
            nc.vector.tensor_scalar(small[2], end, 1.0 / GTEMP, None, ALU.mult).then_inc(dve_step.sem, 1)
            t.eng.wait_ge(dve_step.sem, t.next(dve_step))
            t.alone()
            t.eng.drain().then_inc(dve_to_act.sem, 1)
            for i, (out, src) in enumerate(((GLA_KS, GLA_K), (GLA_K, GLA_K), (GLA_Q, GLA_Q))):
                t.eng.wait_ge(act_to_dve.sem, t.next(act_to_dve))
                last = nc.vector.tensor_tensor(sb(out, T), sb(src, T), sb(GLA_E, T), ALU.mult)
                if i < 2:
                    last.then_inc(dve_to_act.sem, 1)
            barrier(t)
            nc.vector.memset(sb(GLA_B, T), 0.0).then_inc(dve_step.sem, 1)
            t.eng.wait_ge(dve_step.sem, t.next(dve_step))
            t.eng.wait_ge(pe_to_dve.sem, t.next(pe_to_dve))
            t.alone()
            for c in range(QT):
                nc.vector.copy_predicated(sb(GLA_B + c * P, P), con("tri", P).bitcast(mybir.dt.int32), ps(SLOT + c * P, P))
            barrier(t)
            nc.vector.memset(sb(GLA_S, GDV), 0.0).then_inc(dve_step.sem, 1)
            t.eng.wait_ge(dve_step.sem, t.next(dve_step))
            for c in range(QT - 1):
                t.eng.wait_ge(update_done.sem, t.next(update_done))
                nc.vector.scalar_tensor_tensor(sb(GLA_S, GDV), sb(GLA_S, GDV), sb(GLA_SMALL + 24 + c), ps((c % 2) * 512, GDV),
                                               ALU.mult, ALU.add).then_inc(state_ready.sem, 1)
                t.eng.wait_ge(state_ready.sem, t.next(state_ready))
                t.eng.wait_ge(chunk_done.sem, t.next(chunk_done))
                nc.vector.tensor_scalar(sb(GLA_SM, GDV), sb(GLA_S, GDV), sb(GLA_SMALL + 8 + c + 1), None, ALU.mult)\
                    .then_inc(scaled_state.sem, 1)
            t.eng.wait_ge(chunk_done.sem, t.next(chunk_done))
            t.eng.wait_ge(chunk_moved.sem, t.next(chunk_moved, QT))
            nc.vector.tensor_scalar(sb(GLA_SMALL + 40, QT), sb(GLA_SMALL + 40, QT), 1.0 / GDV, LN_EPS, ALU.mult, ALU.add).then_inc(dve_step.sem, 1)
            t.eng.wait_ge(dve_step.sem, t.next(dve_step))
            t.alone()
            t.eng.drain().then_inc(dve_to_act.sem, 1)
            t.eng.wait_ge(act_to_dve.sem, t.next(act_to_dve))
            nc.vector.reciprocal(sb(GLA_SMALL + 48, QT), sb(GLA_SMALL + 40, QT)).then_inc(dve_step.sem, 1)
            t.eng.wait_ge(dve_step.sem, t.next(dve_step))
            for c in range(QT):
                nc.vector.tensor_scalar(sb(GLA_O + c * GDV, GDV), sb(GLA_O + c * GDV, GDV), sb(GLA_SMALL + 48 + c), None, ALU.mult)
            barrier(t)
            for half in range(2):
                t.eng.wait_ge(pe_to_dve.sem, t.next(pe_to_dve))
                gr = sb(h * (2 * T) + (GR_AT + half * T), T)
                nc.vector.scalar_tensor_tensor(gr, ps(half * SLOT, T), sb(h * 2 + (PAR_AT + PB["gla_n"] + half)), gr, ALU.mult, ALU.mult)
            barrier(t)

    def pe_gla_out(t):
        pe_blocks(t, "gla_out", KD, lambda k, c0, n: sb(GR_AT + k * T + c0, n), chunks(T))

    def dve_gla_out(t):
        with t.loop(KD // 2, "gla_out") as i:
            for s in range(2):
                t.eng.wait_ge(block_done[(BLOCKS["gla_out"] + s) % 2].sem, uses(BLOCKS["gla_out"] + s, i, 2))
                m = sb(i * (2 * T) + (MIX_AT + s * T), T)
                nc.vector.tensor_tensor(m, m, ps(s * SLOT, T), ALU.mult).then_inc(psum_free[s].sem, 1)

    DOT_AT = END1

    def dsa_keys(s, c0, n):
        return sb(CL_AT + c0, n)

    def pe_turn_latents(t, s):
        t.eng.wait_ge(o_moved.sem, t.next(o_moved))
        nc.tensor.transpose(ps(OT_PS, P), sb(DOT_AT + s * P, P), con("ident", P)).then_inc(ot_done.sem, 1)

    def pe_dsa(t):
        g = BLOCKS["dsa"]

        def out(s, j):
            t.eng.wait_ge(p_ready[s].sem, t.next(p_ready[s]))
            groups = moves(j + 1)
            for gi, j0, n in groups:
                if gi == 1:
                    t.eng.wait_ge(ot_used.sem, t.next(ot_used))
                if gi == 2:
                    t.eng.wait_ge(t_moved[0].sem, t.next(t_moved[0]))
                for i in range(n):
                    last = nc.tensor.transpose(ps(group_bank(gi) + i * P, P), sb(P_AT + s * TC + (j0 + i) * P, P), con("ident", P))
                last.then_inc(t_done[gi].sem, 1)
            if len(groups) == 1:
                t.eng.wait_ge(ot_used.sem, t.next(ot_used))
            if len(groups) < 3:
                t.eng.wait_ge(t_moved[0].sem, t.next(t_moved[0]))
            if len(groups) > 1:
                t.eng.wait_ge(t_moved[1].sem, t.next(t_moved[1]))
            for i in range(j + 1):
                if i == 6:
                    t.eng.wait_ge(t_moved[2].sem, t.next(t_moved[2]))
                last = nc.tensor.matmul(ps(O_PS, DL), lhsT=sb(PT_AT + s * TC + i * P, P), rhs=sb(CLT_AT + i * P, P), start=i == 0, stop=i == j)
            last.then_inc(o_done.sem, 1)
        with t.loop(DH // 2, "dsa"):
            for s in range(2):
                pe_block(t, g + s, s, x_rhs, chunks(T))
            barrier(t)
            pe_scores(t, 0, P, dsa_keys, P)
            for j in range(QT):
                pe_scores(t, 1, P, dsa_keys, (j + 1) * P)
                out(0, j)
                if j + 1 < QT:
                    pe_scores(t, 0, P, dsa_keys, (j + 2) * P)
                pe_turn_latents(t, 0)
                out(1, j)
                pe_turn_latents(t, 1)
            barrier(t)
            for s in range(2):
                for c0, n in chunks(T):
                    last = nc.tensor.matmul(ps(c0, n, 64 * s, 64 * s + 64), lhsT=sb(HW_AT + s * DHD, DHD), rhs=sb(OL_AT + s * T + c0, n),
                                            start=True, stop=True)
            last.then_inc(pe_to_act.sem, 1)
            barrier(t)

    def act_dsa(t):
        g = BLOCKS["dsa"]
        with t.loop(DH // 2, "dsa") as p:
            nc.scalar.activation(sb(HW_AT, 2 * DHD), sb(p * (2 * DHD) + (PAR_AT + PB["uv"]), 2 * DHD), ACT.Copy)
            for s in range(2):
                t.eng.wait_ge(block_done[(g + s) % 2].sem, uses(g + s, p, 2))
                nc.scalar.activation(sb(QD_AT + s * T, T), ps(s * SLOT, T), ACT.Copy, scale=-DL ** -0.5).then_inc(psum_free[s].sem, 1)
            barrier(t)

            def query(s, j):
                nc.scalar.activation(sb(QS_AT + s * P, P), sb(QD_AT + s * T + j * P, P), ACT.Copy).then_inc(q_ready[s].sem, 1)

            def exp(s, j):
                t.eng.wait_ge(mx_ready[s].sem, t.next(mx_ready[s]))
                nc.scalar.activation(sb(P_AT + s * TC, (j + 1) * P), sb(P_AT + s * TC, (j + 1) * P), ACT.Exp, bias=sb(MX_AT + s),
                                     scale=-1.0, accum_out=sb(SUM_AT + s)).then_inc(p_ready[s].sem, 1)

            def out(s):
                t.eng.wait_ge(o_done.sem, t.next(o_done))
                t.eng.wait_ge(r_ready[s].sem, t.next(r_ready[s]))
                nc.scalar.activation(sb(DOT_AT + s * P, P), ps(O_PS, P), ACT.Copy, scale=sb(RS_AT + s)).then_inc(o_moved.sem, 1)
            query(0, 0)
            query(1, 0)
            exp(0, 0)
            for j in range(QT):
                groups = moves(j + 1)
                if j + 1 < QT:
                    query(0, j + 1)
                if len(groups) > 1:
                    act_move(t, 0, *groups[1])
                exp(1, j)
                out(0)
                if j + 1 < QT:
                    query(1, j + 1)
                if len(groups) > 1:
                    act_move(t, 1, *groups[1])
                if j + 1 < QT:
                    exp(0, j + 1)
                out(1)
            barrier(t)
            t.eng.wait_ge(pe_to_act.sem, t.next(pe_to_act))
            nc.scalar.activation(sb(p * T + GR_AT, T), ps(0, T), ACT.Copy)
            barrier(t)

    def dve_dsa(t):
        with t.loop(DH // 2, "dsa"):
            barrier(t)

            def top(s, j):
                t.eng.wait_ge(s_done[s].sem, t.next(s_done[s]))
                w = (j + 1) * P
                t.alone()
                nc.vector.tensor_tensor_reduce(out=sb(P_AT + s * TC, w), in0=ps(s * SLOT, w), in1=sb(mask_at(j), w), scale=1.0,
                                               scalar=-LOW, op0=ALU.add, op1=ALU.min, accum_out=sb(MX_AT + s)).then_inc(mx_ready[s].sem, 1)

            def latents(s, j):
                t.eng.wait_ge(ot_done.sem, t.next(ot_done))
                nc.vector.tensor_copy(sb(OL_AT + s * T + j * P, P), ps(OT_PS, P)).then_inc(ot_used.sem, 1)
            top(0, 0)
            for j in range(QT):
                groups = moves(j + 1)
                dve_recip(t, 0)
                dve_move(t, 0, *groups[0])
                top(1, j)
                if len(groups) > 2:
                    dve_move(t, 0, *groups[2])
                dve_recip(t, 1)
                if j + 1 < QT:
                    top(0, j + 1)
                latents(0, j)
                dve_move(t, 1, *groups[0])
                if len(groups) > 2:
                    dve_move(t, 1, *groups[2])
                latents(1, j)
            barrier(t)
            barrier(t)

    def pe_mix(t):
        g = BLOCKS["mix"]
        with t.loop(KD, "mix"):
            pe_block(t, g, 0, x_rhs, chunks(T))
            pe_block(t, g + 1, 1, lambda k, c0, n: sb(GR_AT + k * T + c0, n), chunks(T))

    def act_pairs(t, name, func):
        with t.loop(KD, name) as i:
            t.eng.wait_ge(gate_used.sem, t.next(gate_used))
            t.eng.wait_ge(block_done[(BLOCKS[name]) % 2].sem, uses(BLOCKS[name], i, 2))
            nc.scalar.activation(sb(TMP_AT, T), ps(0, T), func).then_inc(psum_free[0].sem, 1)
            t.eng.drain().then_inc(gate_ready.sem, 1)

    def dve_mix(t):
        with t.loop(KD, "mix") as i:
            t.eng.wait_ge(gate_ready.sem, t.next(gate_ready))
            t.eng.wait_ge(block_done[(BLOCKS["mix"] + 1) % 2].sem, uses(BLOCKS["mix"] + 1, i, 2))
            nc.vector.tensor_tensor(sb(TMP_AT, T), sb(TMP_AT, T), ps(SLOT, T), ALU.mult).then_inc(psum_free[1].sem, 1)
            t.eng.drain().then_inc(dve_step.sem, 1)
            t.eng.wait_ge(dve_step.sem, t.next(dve_step))
            m = sb(i * T + MIX_AT, T)
            nc.vector.tensor_tensor(m, m, sb(TMP_AT, T), ALU.add).then_inc(gate_used.sem, 1)

    def dve_residual(t, name, per=2):
        with t.loop(KD // 2, name) as i:
            for s in range(2):
                t.eng.wait_ge(block_done[(BLOCKS[name] + (s + 1) * per // 2 - 1) % 2].sem, uses(BLOCKS[name] + (s + 1) * per // 2 - 1, i, per))
                x = sb(i * (2 * TC) + (X_AT + s * TC), T)
                nc.vector.scalar_tensor_tensor(x, x, ALPHA, ps(s * SLOT, T), ALU.mult, ALU.add).then_inc(psum_free[s].sem, 1)

    def pe_layer_norm(t, at, stride):
        for k in range(KD):
            for c0, n in chunks(T):
                last = nc.tensor.matmul(ps(c0, n), lhsT=con("ones", P), rhs=sb(at + k * stride + c0, n), start=k == 0, stop=k == KD - 1)
        last.then_inc(pe_to_dve.sem, 1)
        for k in range(KD):
            s = t.tiles % 2
            t.tiles += 1
            t.eng.wait_ge(squares[s].sem, t.next(squares[s]))
            for c0, n in chunks(T):
                last = nc.tensor.matmul(ps(SLOT + c0, n), lhsT=con("ones", P), rhs=sb(TMP_AT + s * TC + c0, n), start=k == 0, stop=k == KD - 1)
            last.then_inc(squares_used[s].sem, 1)
        t.eng.wait_ge(var_ready.sem, t.next(var_ready))

    def act_layer_norm(t, at, stride, gain, bias):
        for k in range(KD):
            t.eng.wait_ge(dve_to_act.sem, t.next(dve_to_act))
            s = t.tiles % 2
            t.tiles += 1
            t.eng.wait_ge(squares_used[s].sem, t.next(squares_used[s]))
            nc.scalar.activation(sb(TMP_AT + s * TC, T), sb(at + k * stride, T), ACT.Square).then_inc(squares[s].sem, 1)
        act_root(t, T)
        for k in range(KD):
            t.eng.wait_ge(scaled.sem, t.next(scaled))
            x = sb(at + k * stride, T)
            nc.scalar.activation(x, x, ACT.Identity, scale=par(gain, off=k), bias=par(bias, off=k))

    def dve_layer_norm(t, at, stride):
        t.eng.wait_ge(pe_to_dve.sem, t.next(pe_to_dve))
        nc.vector.tensor_scalar(sb(STAT_AT, T), ps(0, T), 1.0 / D, None, ALU.mult).then_inc(dve_step.sem, 1)
        t.eng.wait_ge(dve_step.sem, t.next(dve_step))
        for k in range(KD):
            x = sb(at + k * stride, T)
            nc.vector.tensor_tensor(x, x, sb(STAT_AT, T), ALU.subtract).then_inc(dve_to_act.sem, 1)
        t.eng.drain().then_inc(dve_step.sem, 1)
        t.eng.wait_ge(dve_step.sem, t.next(dve_step))
        dve_rstd(t, D, LN_EPS, SLOT, T, KD)
        for k in range(KD):
            x = sb(at + k * stride, T)
            nc.vector.tensor_tensor(x, x, sb(STAT_AT, T), ALU.mult).then_inc(scaled.sem, 1)

    def pe_up(t):
        g = BLOCKS["up"]
        with t.loop(KF, "up"):
            for s in range(2):
                pe_block(t, g + s, s, x_rhs, chunks(T))

    def act_up(t):
        nc.scalar.preload_act_table(ACT.Silu)
        with t.loop(KF, "up") as i:
            for s in range(2):
                t.eng.wait_ge(h_used[s].sem, t.next(h_used[s]))
                t.eng.wait_ge(block_done[(BLOCKS["up"] + s) % 2].sem, uses(BLOCKS["up"] + s, i, 2))
                nc.scalar.activation(sb(HG_AT + s * T, T), ps(s * SLOT, T), ACT.Identity,
                                     scale=sb(i + (PAR_AT + PB["cw"] + 2 * 2 * KF + s * KF)),
                                     bias=sb(i + (PAR_AT + PB["cb"] + s * KF))).then_inc(h_ready[s].sem, 1)
                if s:
                    t.eng.wait_ge(gate_convolved.sem, t.next(gate_convolved))
                    nc.scalar.activation(sb(HG_AT, T), sb(HG_AT, T), ACT.Silu).then_inc(silu_ready.sem, 1)

    def dve_up(t):
        for s in range(2):
            nc.vector.memset(sb(SMALL_AT + 8 + s), 0.0).then_inc(h_used[s].sem, 1)
        t.eng.wait_ge(h_used[0].sem, t.next(h_used[0]))
        with t.loop(KF, "up") as i:
            for s in range(2):
                t.eng.wait_ge(h_ready[s].sem, t.next(h_ready[s]))
                t.eng.wait_ge(block_done[(BLOCKS["up"] + s) % 2].sem, uses(BLOCKS["up"] + s, i, 2))
                for back in (1, 2):
                    h = sb(HG_AT + s * T + back, T - back)
                    w = sb(i + (PAR_AT + PB["cw"] + (2 - back) * 2 * KF + s * KF))
                    nc.vector.scalar_tensor_tensor(h, ps(s * SLOT, T - back), w, h, ALU.mult, ALU.add).then_inc(dve_step.sem, 1)
                    t.eng.wait_ge(dve_step.sem, t.next(dve_step))
                t.alone()
                t.eng.drain().then_inc(psum_free[s].sem, 1)
                if s == 0:
                    t.eng.drain().then_inc(gate_convolved.sem, 1)
            t.eng.wait_ge(silu_ready.sem, t.next(silu_ready))
            nc.vector.tensor_tensor(sb(i * T + A_AT, T), sb(HG_AT, T), sb(HG_AT + T, T), ALU.mult).then_inc(h_used[0].sem, 1)
            t.eng.drain().then_inc(h_used[1].sem, 1)
            t.eng.wait_ge(h_used[0].sem, t.next(h_used[0]))

    def pe_down(t):
        with t.loop(KD // 2, "down"):
            for s in range(2):
                t.eng.wait_ge(psum_free[s].sem, t.next(psum_free[s]))
                for b in range(3):
                    w = (3 * s + b) % 2
                    t.eng.wait_ge(w_loaded[w].sem, t.next(w_loaded[w]))
                    tiles = min(KD, KF - b * KD)
                    for c0, n in chunks(T):
                        for k in range(tiles):
                            last = nc.tensor.matmul(ps(s * SLOT + c0, n), lhsT=sb(W_AT + w * 1024 + k * P, P),
                                                    rhs=sb(A_AT + (b * KD + k) * T + c0, n), start=b == 0 and k == 0,
                                                    stop=b == 2 and k == tiles - 1)
                    last.then_inc(block_done[w].sem, 1)

    Z_AT = A_AT

    def pe_ple(t):
        g = BLOCKS["ple"]
        t.eng.wait_ge(p_in.sem, t.next(p_in))
        with t.loop(KD, "ple"):
            pe_block(t, g, 0, x_rhs, chunks(T))
            pe_block(t, g + 1, 1, lambda k, c0, n: sb(PT_IN_AT + k * T + c0, n), chunks(T), nk=PLE // P)

    def dve_ple(t):
        with t.loop(KD, "ple") as i:
            t.eng.wait_ge(gate_ready.sem, t.next(gate_ready))
            t.eng.wait_ge(block_done[(BLOCKS["ple"] + 1) % 2].sem, uses(BLOCKS["ple"] + 1, i, 2))
            nc.vector.tensor_tensor(sb(TMP_AT, T), sb(TMP_AT, T), ps(SLOT, T), ALU.mult).then_inc(psum_free[1].sem, 1)
            t.eng.drain().then_inc(dve_step.sem, 1)
            t.eng.wait_ge(dve_step.sem, t.next(dve_step))
            nc.vector.scalar_tensor_tensor(sb(i * T + Z_AT, T), sb(i * TC + X_AT, T), ALPHA, sb(TMP_AT, T), ALU.mult, ALU.add)\
                .then_inc(gate_used.sem, 1)

    SECOND = [
        ("final", pe_final, act_final, dve_final),
        ("index_proj", lambda t: pe_blocks(t, "index", 6, x_rhs, chunks(T)), act_index_proj, None),
        ("latents", pe_latents, act_latents, dve_latents),
        ("index", pe_scores_index, act_scores_index, dve_scores_index),
        ("select", pe_gates, act_gates, dve_select),
        ("gla", pe_gla, act_gla, dve_gla),
        ("gla_out", pe_gla_out, None, dve_gla_out),
        ("dsa", pe_dsa, act_dsa, dve_dsa),
        ("mix", pe_mix, lambda t: act_pairs(t, "mix", ACT.Sigmoid), dve_mix),
        ("out2", lambda t: pe_blocks(t, "out2", KD, lambda k, c0, n: sb(MIX_AT + k * T + c0, n), chunks(T)), None,
         lambda t: dve_residual(t, "out2")),
        ("ln1", lambda t: pe_layer_norm(t, X_AT, TC), lambda t: act_layer_norm(t, X_AT, TC, "ln1g", "ln1b"),
         lambda t: dve_layer_norm(t, X_AT, TC)),
        ("up", pe_up, act_up, dve_up),
        ("down", pe_down, None, lambda t: dve_residual(t, "down", 6)),
        ("ln2", lambda t: pe_layer_norm(t, X_AT, TC), lambda t: act_layer_norm(t, X_AT, TC, "ln2g", "ln2b"),
         lambda t: dve_layer_norm(t, X_AT, TC)),
        ("ple", pe_ple, lambda t: act_pairs(t, "ple", ACT.Sigmoid), dve_ple),
        ("ln3", lambda t: pe_layer_norm(t, Z_AT, T), lambda t: act_layer_norm(t, Z_AT, T, "ln3g", "ln3b"),
         lambda t: dve_layer_norm(t, Z_AT, T)),
    ]

    def second_block(t, which):
        for name, *steps in SECOND:
            if steps[which]:
                steps[which](t)
            barrier(t)
            if name == "dsa" and which == 2:
                t.eng.drain().then_inc(sparse_done.sem, 1)

    @block.sync
    def _(eng):
        t = Track(eng, "sp")
        for s in range(2):
            eng.dma_start(sb(W_AT + s * 1024, 1024), io["stream"][s]).then_inc(w_loaded[s].sem, 16)
        with t.loop(NBLOCKS // 2 - 1, "stream") as i:
            for s in range(2):
                t.eng.wait_ge(block_done[s].sem, t.next(block_done[s]))
                eng.dma_start(sb(W_AT + s * 1024, 1024), io["stream"][bass.ds(i * 2 + (s + 2), 1)].rearrange("a p n -> (a p) n"))\
                    .then_inc(w_loaded[s].sem, 16)
        for s in range(2):
            eng.wait_ge(w_loaded[s].sem, 16 * (NBLOCKS // 2))

    @block.gpsimd
    def _(eng):
        t = Track(eng, "pool")
        eng.dma_start(sb(CON_AT, NCON), io["consts"]).then_inc(consts_in.sem, 16)
        eng.dma_start(sb(PAR_AT, NPA), io["par_a"][0]).then_inc(params_in.sem, 16)
        for k in range(KD):
            eng.dma_start(sb(H_AT + k * TC, TC), io["x0"][:, k * TC:(k + 1) * TC]).then_inc(x_in.sem, 16)
        eng.dma_start(sb(TAB_AT, NTAB), io["tables"]).then_inc(tables_in.sem, 16)
        for l in range(LAYERS):
            if l:
                t.eng.wait_ge(x_out.sem, t.next(x_out, KD))
            pool_layer(t, l)
        t.eng.wait_ge(sparse_done.sem, t.next(sparse_done))
        eng.dma_start(sb(PT_IN_AT, 2 * T), io["p"]).then_inc(p_in.sem, 16)
        t.eng.wait_ge(finished.sem, t.next(finished))
        eng.dma_start(io["out"], sb(Z_AT, KD * T)).then_inc(stored.sem, 16)
        t.eng.wait_ge(stored.sem, t.next(stored))

    @block.tensor
    def _(eng):
        t = Track(eng, "pe", pe_step, waited["pe"])
        pe_mod(t)
        barrier(t)
        for l in range(LAYERS):
            for step in (pe_norm, pe_project, pe_conv, pe_head_norms, pe_rope):
                step(t, l)
                barrier(t)
            pe_mla(t, l)
            pe_gqa(t, l)
            barrier(t)
            pe_outproj(t, l)
            barrier(t)
        second_block(t, 0)

    @block.scalar
    def _(eng):
        t = Track(eng, "act", act_step, waited["act"])
        act_mod(t)
        barrier(t)
        for l in range(LAYERS):
            for step in (act_norm, act_project, act_conv, act_head_norms, act_rope):
                step(t, l)
                barrier(t)
            act_mla(t, l)
            act_gqa(t, l)
            barrier(t)
            barrier(t)
        second_block(t, 1)

    @block.vector
    def _(eng):
        t = Track(eng, "dve", dve_step, waited["dve"])
        for n, ev in enumerate((psum_free[0], psum_free[1], ot_used, gate_used)):
            nc.vector.memset(sb(SMALL_AT + 8 + n), 0.0).then_inc(ev.sem, 1)
        dve_mod(t)
        barrier(t)
        for l in range(LAYERS):
            for step in (dve_norm, dve_project, dve_conv, dve_head_norms):
                step(t, l)
                barrier(t)
            if l == 0:
                t.eng.wait_ge(tables_in.sem, t.next(tables_in))
            dve_rope(t, l)
            barrier(t)
            dve_mla(t, l)
            dve_gqa(t, l)
            barrier(t)
            eng.drain().then_inc(attended.sem, 1)
            dve_outproj(t, l)
            barrier(t)
        second_block(t, 2)
        eng.drain().then_inc(finished.sem, 1)

    hold.close()



def rope_tables():
    def table(dim):
        half = dim // 4
        freqs = THETA ** (-np.arange(half, dtype=np.float32) / np.float32(half))
        row, col = np.repeat(np.arange(T // GRID_W), GRID_W), np.tile(np.arange(GRID_W), T // GRID_W)
        rows = []
        for pos in (row, col):
            angle = (pos.astype(np.float32)[None, :] * freqs[:, None].astype(np.float32))
            rows += [angle, angle]
        a = np.concatenate(rows).astype(np.float32)
        return np.cos(a), np.sin(a)
    out = np.zeros((P, NTAB), np.float32)
    c, s = table(MROPE)
    out[64:96, TAB["mla_cos"]:TAB["mla_cos"] + T], out[64:96, TAB["mla_sin"]:TAB["mla_sin"] + T] = c, s
    c, s = table(GD)
    out[:, TAB["gqa_cos"]:TAB["gqa_cos"] + T], out[:, TAB["gqa_sin"]:TAB["gqa_sin"] + T] = np.tile(c, (2, 1)), np.tile(s, (2, 1))
    return out


def turn_matrix(dim):
    q = dim // 4
    m = np.zeros((dim, dim), np.float32)
    for base in (0, 2 * q):
        for j in range(q):
            m[base + q + j, base + j] = -1.0
            m[base + j, base + q + j] = 1.0
    return m


def feature_tiles(v):
    return np.asarray(v).reshape(-1, P).T


def pack_consts(i):
    out = np.zeros((P, NCON), np.float32)
    def put(name, a, p0=0):
        out[p0:p0 + a.shape[0], CON[name]:CON[name] + a.shape[1]] = a
    put("ident", np.eye(P, dtype=np.float32))
    put("ones", np.ones((P, P), np.float32))
    put("halves", np.kron(np.eye(2, dtype=np.float32), np.ones((64, 64), np.float32)))
    put("turn_mla", turn_matrix(MROPE), 64)
    put("turn_gqa", np.kron(np.eye(2, dtype=np.float32), turn_matrix(GD)))
    put("tri", np.triu(np.ones((P, P), np.float32)))
    put("later", np.triu(np.full((P, P), -NEG, np.float32), 1))
    put("b_mod", np.concatenate([feature_tiles(i["b_mod"][l]) for l in range(LAYERS)], 1))
    put("final_w", feature_tiles(i["final_norm_w"]))
    put("vec", np.stack([feature_tiles(i["c"][0]), feature_tiles(i["c_ctx"])], -1).reshape(P, -1))
    return out


def pack_layer(i, l):
    out = np.zeros((P, NPA), np.float32)
    def put(name, a, off=0):
        out[:a.shape[0], PA[name] + off:PA[name] + off + a.shape[1]] = a
    uq = i["mla_w_uq"][l].reshape(2, P, MH, MQ)
    ukv = i["mla_w_ukv"][l].reshape(P, MH, MNOPE + MV)
    for h in range(MH):
        for k in range(2):
            put("uqk", uq[k, :, h], h * 256 + k * MQ)
        put("uqk", ukv[:, h, :MNOPE], h * 256 + 2 * MQ)
        put("uv", ukv[:, h, MNOPE:], h * MV)
    put("dw", i["conv_dw_w"][l].reshape(CK, 2, P).transpose(2, 0, 1).reshape(P, -1))
    for name, src in (("dwb", "conv_dw_b"), ("lnw", "conv_ln_w"), ("lnb", "conv_ln_b"), ("pwb", "conv_pw_b"),
                      ("nw", "norm_w"), ("qn", "mla_q_norm"), ("kvn", "mla_kv_norm")):
        put(name, feature_tiles(i[src][l]))
    put("pw", i["conv_pw_w"][l].reshape(2, P, CC).transpose(1, 0, 2).reshape(P, -1))
    for name, src in (("gqn", "gqa_q_norm"), ("gkn", "gqa_k_norm")):
        put(name, np.tile(i[src][l], 2)[:, None])
    return out


def pack_stream(i):
    out = np.zeros((NBLOCKS, P, 1024), np.float32)
    at = [0]

    def add(a):
        out[at[0], :a.shape[0], :a.shape[1]] = a
        at[0] += 1
    for l in range(LAYERS):
        for j in range(24):
            add(column_block(i["w_mod"][l], j * P))
    q, kv, kr, gk, gv, gq, conv, gate = first_columns()
    order = mix_order()
    for l in range(LAYERS):
        w = i["w_in"][l]
        assert at[0] == BLOCKS[f"kv{l}"]
        add(column_block(w, kv))
        padded = np.zeros((D, P), np.float32)
        padded[:, 64:96] = w[:, kr:kr + MROPE]
        add(column_block(padded, 0))
        for c in (gk, gv, q, q + P):
            add(column_block(w, c))
        for p in range(3):
            heads = GQA_ORDER[2 * p:2 * p + 2]
            add(column_block(w, np.concatenate([np.arange(gq + 64 * h, gq + 64 * h + 64) for h in heads])))
        for c in (conv + 256, conv, conv + 256 + P, conv + P):
            add(column_block(w, c))
        for m in range(KD):
            add(column_block(w, gate + order[m * P:(m + 1) * P]))
        for m in range(KD):
            add(column_block(i["w_out"][l][order], m * P))
    w, at2 = i["w_in_2"][0], second_columns()
    assert at[0] == BLOCKS["index"]
    for j in range(4):
        add(column_block(w, at2["iq"] + j * P))
    add(column_block(w, at2["ckv"]))
    padded = np.zeros((D, P), np.float32)
    padded[:, 0:64] = w[:, at2["ik"]:at2["ik"] + 64]
    padded[:, 64:64 + GRANK] = w[:, at2["ga"]:at2["ga"] + GRANK]
    padded[:, 96:96 + IH] = w[:, at2["iw"]:at2["iw"] + IH]
    add(column_block(padded, 0))
    for m in range(KD):
        add(column_block(w, at2["gates"] + m * P))
    for m in range(KD):
        add(column_block(w, at2["gr"] + m * P))
    for h in range(GLH):
        for c in (at2["gq"] + h * P, at2["gk"] + h * P, at2["gv"] + h * GDV, at2["gv"] + h * GDV + P):
            add(column_block(w, c))
    for m in range(KD):
        add(column_block(i["w_gla_proj_2"][0], m * P))
    for h in range(DH):
        add(column_block(w, at2["dq"] + h * P))
    for m in range(KD):
        add(column_block(w, at2["gates"] + D + m * P))
        add(column_block(i["w_dsa_proj_2"][0], m * P))
    for m in range(KD):
        add(column_block(i["w_out_2"][0], m * P))
    for m in range(KF):
        add(column_block(i["w_up_2"][0], m * P))
        add(column_block(i["w_up_2"][0], FF + m * P))
    for m in range(KD):
        down = column_block(i["w_down_2"][0], m * P)
        for k in range(0, KF, KD):
            add(down[:, k * P:(k + KD) * P])
    for m in range(KD):
        add(column_block(i["w_ple_gate_2"][0], m * P))
        add(column_block(i["w_ple_2"][0], m * P))
    assert at[0] == NBLOCKS
    return out


def tokens_last(a):
    return a.T.reshape(-1, P, a.shape[0]).transpose(1, 0, 2)


def pack_second(i):
    out = np.zeros((P, NPB), np.float32)

    def put(name, a, off=0, p0=0):
        out[p0:p0 + a.shape[0], PB[name] + off:PB[name] + off + a.shape[1]] = a
    put("gate_up", i["w_gla_gate_up_2"][0], 0, 64)
    put("uv", i["w_uv_2"][0].transpose(1, 0, 2).reshape(DL, -1))
    for j in range(3):
        put("cw", feature_tiles(i["conv_w_2"][0, j]), j * 2 * KF)
    for name, src in (("b_gate", "b_gla_gate_2"), ("gla_n", "g_gla_norm_2"), ("ckv_n", "g_ckv_norm_2"), ("cb", "conv_b_2"),
                      ("ln1g", "ln1_g_2"), ("ln1b", "ln1_b_2"), ("ln2g", "ln2_g_2"), ("ln2b", "ln2_b_2"),
                      ("ln3g", "ln3_g_2"), ("ln3b", "ln3_b_2")):
        put(name, feature_tiles(i[src][0]))
    return out


def host_arrays(i):
    x0 = np.concatenate([tokens_last(i["x"][0]), tokens_last(i["ctx"][0])], 2)
    return {"x0": x0.reshape(P, -1), "stream": pack_stream(i), "consts": pack_consts(i),
            "par_b": pack_second(i), "p": tokens_last(i["p_2"][0, 0]).reshape(P, -1), "tables": rope_tables(),
            "par_a": np.stack([pack_layer(i, l) for l in range(LAYERS)])}


def kernel(**inputs):
    import numpy as _np
    import concourse.bacc as _bacc
    from concourse import mybir as _mybir
    from concourse.bass_utils import run_bass_kernel_spmd as _run

    arrays = {name: _np.ascontiguousarray(a) for name, a in host_arrays(inputs).items()}
    nc = _bacc.Bacc("TRN2", target_bir_lowering=False, num_devices=1)
    io = {name: nc.dram_tensor(name, a.shape, _mybir.dt.float32, kind="ExternalInput").ap() for name, a in arrays.items()}
    io["x_mid"] = nc.dram_tensor("x_mid", (P, KD * TC), _mybir.dt.float32, kind="Internal").ap()
    io["out"] = nc.dram_tensor("out", (P, KD * T), _mybir.dt.float32, kind="ExternalOutput").ap()
    program(nc, io)
    r = _run(nc, [arrays], core_ids=[0])
    return r.results[0]["out"].reshape(P, KD, T).transpose(2, 1, 0).reshape(1, T, D)
```
